# Optimizing a Trainium2 kernel written in Bass

```python
import math
import jax, jax.numpy as jnp
from jax import lax
import numpy as np

D_MODEL = 1024
BATCH = 1
SEQ = 512
DEPTH = 2
DEC_BATCH = 1
DEC_SEQ = 32
PAST_LEN = 256

CHUNK = 64
Q_BLOCK = 128
N_HEADS = 8
HEAD_DIM = 64
V_DIM = 2 * HEAD_DIM
ATTN_QK = N_HEADS * HEAD_DIM
ATTN_V = N_HEADS * V_DIM
D_LRU = D_MODEL
LRU_BLOCKS = 16
LRU_BW = D_LRU // LRU_BLOCKS
CONV_W = 4
LRU_C = 8.0
D_FF = 4 * D_MODEL
EPS = 1e-6
NEG = -1e30
IN_SIZES = (ATTN_QK, ATTN_QK, ATTN_QK, ATTN_QK, ATTN_V, D_LRU, D_LRU, D_MODEL, D_MODEL)
D_IN = 4 * ATTN_QK + ATTN_V + 2 * D_LRU + 2 * D_MODEL

kernel_name = "hybrid_diffattn_rglru_streaming_step"

def _rms(x, g):
    x32 = x.astype(jnp.float32)
    y = x32 * lax.rsqrt(jnp.mean(x32 * x32, axis=-1, keepdims=True) + EPS) * g.astype(jnp.float32)
    return y.astype(x.dtype)

def _alibi_slopes():
    i = jnp.arange(1, N_HEADS + 1, dtype=jnp.float32)
    return jnp.exp2(-8.0 * i / N_HEADS)

def _diff_attn(q1, q2, k1, k2, v, q_pos, k_pos, lam):
    scale = HEAD_DIM ** -0.5
    dist = jnp.abs(q_pos[:, None] - k_pos[None, :]).astype(jnp.float32)
    bias = -_alibi_slopes()[:, None, None] * dist[None]
    allowed = (k_pos[None, :] // CHUNK) <= (q_pos[:, None] // CHUNK)
    bias = jnp.where(allowed[None], bias, NEG)
    s1 = jnp.einsum('bqhd,bkhd->bhqk', q1, k1).astype(jnp.float32) * scale + bias
    s2 = jnp.einsum('bqhd,bkhd->bhqk', q2, k2).astype(jnp.float32) * scale + bias
    p = jax.nn.softmax(s1, axis=-1) - lam * jax.nn.softmax(s2, axis=-1)
    return jnp.einsum('bhqk,bkhd->bqhd', p.astype(v.dtype), v)

def _prompt_attn(q1, q2, k1, k2, v, lam):
    B, S = q1.shape[:2]
    nb = S // Q_BLOCK
    pos = jnp.arange(S, dtype=jnp.int32)

    def to_blocks(t):
        return jnp.swapaxes(t.reshape(B, nb, Q_BLOCK, N_HEADS, HEAD_DIM), 0, 1)

    def blk(args):
        a1, a2, qp = args
        return _diff_attn(a1, a2, k1, k2, v, qp, pos, lam)

    out = lax.map(blk, (to_blocks(q1), to_blocks(q2), pos.reshape(nb, Q_BLOCK)))
    return jnp.swapaxes(out, 0, 1).reshape(B, S, N_HEADS, V_DIM)

def _causal_conv(x, buf, w, b):
    T = x.shape[1]
    xp = jnp.concatenate([buf.astype(x.dtype), x], axis=1)
    y = sum(xp[:, j:j + T] * w[j] for j in range(CONV_W)) + b
    return y, xp[:, -(CONV_W - 1):]

def _rg_lru(x, w_r, b_r, w_i, b_i, lam_param, h0):
    B, T, _ = x.shape
    xb = x.reshape(B, T, LRU_BLOCKS, LRU_BW)
    r_gate = jax.nn.sigmoid((jnp.einsum('btnc,ncd->btnd', xb, w_r).reshape(B, T, D_LRU) + b_r).astype(jnp.float32))
    i_gate = jax.nn.sigmoid((jnp.einsum('btnc,ncd->btnd', xb, w_i).reshape(B, T, D_LRU) + b_i).astype(jnp.float32))
    log_a = -LRU_C * r_gate * jax.nn.softplus(-lam_param.astype(jnp.float32))
    a = jnp.exp(log_a)
    u = jnp.sqrt(-jnp.expm1(2.0 * log_a)) * (i_gate * x.astype(jnp.float32))
    u = u.at[:, 0].add(a[:, 0] * h0.astype(jnp.float32))

    def comb(left, right):
        a1, b1 = left
        a2, b2 = right
        return a1 * a2, a2 * b1 + b2

    _, h = lax.associative_scan(comb, (a, u), axis=1)
    return h.astype(x.dtype), h[:, -1]

def _layer(x, l, p, k_past, v_past, conv_buf, h0):
    B, T, _ = x.shape
    lam_init = 0.8 - 0.6 * math.exp(-0.3 * l)
    h = _rms(x, p['g_mix_pre'])
    proj = h @ p['w_in']
    idx = np.cumsum(IN_SIZES)[:-1].tolist()
    q1, q2, k1, k2, v, ux, ug, ga, gb = jnp.split(proj, idx, axis=-1)
    q1 = q1.reshape(B, T, N_HEADS, HEAD_DIM)
    q2 = q2.reshape(B, T, N_HEADS, HEAD_DIM)
    k1 = k1.reshape(B, T, N_HEADS, HEAD_DIM)
    k2 = k2.reshape(B, T, N_HEADS, HEAD_DIM)
    v = v.reshape(B, T, N_HEADS, V_DIM)
    lq1 = p['lambda_q1'].astype(jnp.float32); lk1 = p['lambda_k1'].astype(jnp.float32)
    lq2 = p['lambda_q2'].astype(jnp.float32); lk2 = p['lambda_k2'].astype(jnp.float32)
    lam = jnp.exp(jnp.sum(lq1 * lk1)) - jnp.exp(jnp.sum(lq2 * lk2)) + lam_init
    k_rows = jnp.concatenate([k1, k2], axis=2)
    if k_past is None:
        o = _prompt_attn(q1, q2, k1, k2, v, lam)
    else:
        P = k_past.shape[1]
        K = jnp.concatenate([k_past.astype(x.dtype), k_rows], axis=1)
        V = jnp.concatenate([v_past.astype(x.dtype), v], axis=1)
        q_pos = P + jnp.arange(T, dtype=jnp.int32)
        k_pos = jnp.arange(P + T, dtype=jnp.int32)
        o = _diff_attn(q1, q2, K[:, :, :N_HEADS], K[:, :, N_HEADS:], V, q_pos, k_pos, lam)
    o = _rms(o, p['g_sub']) * (1.0 - lam_init)
    branch_a = o.reshape(B, T, ATTN_V) @ p['w_branch_attn']
    uc, conv_new = _causal_conv(ux, conv_buf, p['conv_w'], p['conv_b'])
    hl, h_last = _rg_lru(uc, p['w_rg'], p['b_rg'], p['w_ig'], p['b_ig'], p['lru_lambda'], h0)
    branch_b = (hl * jax.nn.gelu(ug)) @ p['w_branch_lru']
    m = jax.nn.sigmoid(ga) * branch_a + jax.nn.sigmoid(gb) * branch_b
    x = x + _rms(m @ p['w_out'], p['g_mix_post'])
    f = jnp.square(jax.nn.relu(_rms(x, p['g_mlp_pre']) @ p['w_up'])) @ p['w_down']
    x = x + _rms(f, p['g_mlp_post'])
    return x, k_rows, v, conv_new, h_last

def setup_inputs(seed: int = 0) -> dict:
    key = jax.random.key(seed)
    ks = jax.random.split(key, 32)
    f32 = jnp.float32
    nrm = lambda k, s, sc: jax.random.normal(k, s, f32) * sc
    gain = lambda k, s: 1.0 + 0.05 * jax.random.normal(k, s, f32)
    u = jax.random.uniform(ks[20], (DEPTH, D_LRU), f32, 0.9, 0.999)
    a_base = u ** (1.0 / LRU_C)
    lru_lambda = jnp.log(a_base) - jnp.log1p(-a_base)
    return {
        'x_prompt': nrm(ks[0], (BATCH, SEQ, D_MODEL), 1.0),
        'x_sample': nrm(ks[1], (DEC_BATCH, DEC_SEQ, D_MODEL), 1.0),
        'cache_k': nrm(ks[2], (DEPTH, DEC_BATCH, PAST_LEN, 2 * N_HEADS, HEAD_DIM), 1.0),
        'cache_v': nrm(ks[3], (DEPTH, DEC_BATCH, PAST_LEN, N_HEADS, V_DIM), 1.0),
        'state_conv': nrm(ks[4], (DEPTH, DEC_BATCH, CONV_W - 1, D_LRU), 1.0),
        'state_lru': nrm(ks[5], (DEPTH, DEC_BATCH, D_LRU), 0.5),
        'w_in': nrm(ks[6], (DEPTH, D_MODEL, D_IN), D_MODEL ** -0.5),
        'lambda_q1': nrm(ks[7], (DEPTH, HEAD_DIM), 0.1),
        'lambda_k1': nrm(ks[8], (DEPTH, HEAD_DIM), 0.1),
        'lambda_q2': nrm(ks[9], (DEPTH, HEAD_DIM), 0.1),
        'lambda_k2': nrm(ks[10], (DEPTH, HEAD_DIM), 0.1),
        'g_sub': gain(ks[11], (DEPTH, V_DIM)),
        'conv_w': nrm(ks[12], (DEPTH, CONV_W, D_LRU), CONV_W ** -0.5),
        'conv_b': nrm(ks[13], (DEPTH, D_LRU), 0.01),
        'w_rg': nrm(ks[14], (DEPTH, LRU_BLOCKS, LRU_BW, LRU_BW), LRU_BW ** -0.5),
        'b_rg': nrm(ks[15], (DEPTH, D_LRU), 0.01),
        'w_ig': nrm(ks[16], (DEPTH, LRU_BLOCKS, LRU_BW, LRU_BW), LRU_BW ** -0.5),
        'b_ig': nrm(ks[17], (DEPTH, D_LRU), 0.01),
        'lru_lambda': lru_lambda,
        'w_branch_attn': nrm(ks[18], (DEPTH, ATTN_V, D_MODEL), ATTN_V ** -0.5),
        'w_branch_lru': nrm(ks[19], (DEPTH, D_LRU, D_MODEL), D_LRU ** -0.5),
        'w_out': nrm(ks[21], (DEPTH, D_MODEL, D_MODEL), D_MODEL ** -0.5),
        'w_up': nrm(ks[22], (DEPTH, D_MODEL, D_FF), D_MODEL ** -0.5),
        'w_down': nrm(ks[23], (DEPTH, D_FF, D_MODEL), D_FF ** -0.5),
        'g_mix_pre': gain(ks[24], (DEPTH, D_MODEL)),
        'g_mix_post': gain(ks[25], (DEPTH, D_MODEL)),
        'g_mlp_pre': gain(ks[26], (DEPTH, D_MODEL)),
        'g_mlp_post': gain(ks[27], (DEPTH, D_MODEL)),
    }

def reference(x_prompt, x_sample, cache_k, cache_v, state_conv, state_lru,
              w_in, lambda_q1, lambda_k1, lambda_q2, lambda_k2, g_sub,
              conv_w, conv_b, w_rg, b_rg, w_ig, b_ig, lru_lambda,
              w_branch_attn, w_branch_lru, w_out, w_up, w_down,
              g_mix_pre, g_mix_post, g_mlp_pre, g_mlp_post):
    xp, xs = x_prompt, x_sample
    pk, pv, pc, pl = [], [], [], []
    sk, sv, sc, sl = [], [], [], []
    for l in range(DEPTH):
        p = dict(w_in=w_in[l], lambda_q1=lambda_q1[l], lambda_k1=lambda_k1[l],
                 lambda_q2=lambda_q2[l], lambda_k2=lambda_k2[l], g_sub=g_sub[l],
                 conv_w=conv_w[l], conv_b=conv_b[l], w_rg=w_rg[l], b_rg=b_rg[l],
                 w_ig=w_ig[l], b_ig=b_ig[l], lru_lambda=lru_lambda[l],
                 w_branch_attn=w_branch_attn[l], w_branch_lru=w_branch_lru[l],
                 w_out=w_out[l], w_up=w_up[l], w_down=w_down[l],
                 g_mix_pre=g_mix_pre[l], g_mix_post=g_mix_post[l],
                 g_mlp_pre=g_mlp_pre[l], g_mlp_post=g_mlp_post[l])
        Bp = xp.shape[0]
        zero_buf = jnp.zeros((Bp, CONV_W - 1, D_LRU), xp.dtype)
        zero_h = jnp.zeros((Bp, D_LRU), jnp.float32)
        xp, k_r, v_r, c_n, h_n = _layer(xp, l, p, None, None, zero_buf, zero_h)
        pk.append(k_r); pv.append(v_r); pc.append(c_n); pl.append(h_n)
        xs, k_r, v_r, c_n, h_n = _layer(xs, l, p, cache_k[l], cache_v[l], state_conv[l], state_lru[l])
        sk.append(k_r); sv.append(v_r); sc.append(c_n); sl.append(h_n)
    return (xp, xs,
            jnp.stack(pk), jnp.stack(pv), jnp.stack(pc), jnp.stack(pl),
            jnp.stack(sk), jnp.stack(sv), jnp.stack(sc), jnp.stack(sl))


_drawn_inputs = setup_inputs


def setup_inputs(seed=0):
    import zlib

    import numpy as np

    out = dict(_drawn_inputs(seed))
    spreads = {}
    factors = {'lambda_q2': 3.328, 'b_rg': 29.665, 'b_ig': 8.0}
    for name, (base, spread) in spreads.items():
        noise = np.random.default_rng([zlib.crc32(name.encode()), seed]).standard_normal(out[name].shape)
        drawn = base * np.exp(spread * noise) if base else spread * noise
        out[name] = __import__('jax').numpy.asarray(drawn.astype(out[name].dtype))
    for name, factor in factors.items():
        out[name] = (out[name] * factor).astype(out[name].dtype)
    return out
```

```python
import math
from contextlib import ExitStack

import concourse.bass as bass
from concourse import mybir

P = 128
ALU = mybir.AluOpType
ACT = mybir.ActivationFunctionType
F32 = mybir.dt.float32
F32R = mybir.dt.float32r

EPS = 1e-6
NHEAD = 8
HD = 64
VD = 128
CHUNK = 64
SCALE = HD ** -0.5
KT = 8
NS = 32
NP_ = 512
NT = NS + NP_
HT = NT // 2
PAST = 256
NKS = PAST + NS
CW = 4
LW = 548
LH = LW // 2
PR = 35
WR = 4
TL = 144
T_GB, T_WA, T_WL, T_WO, T_MLP = 48, 56, 64, 72, 80
(R_GPRE, R_GPOST, R_MPRE, R_MPOST, R_CW, R_CB, R_BR, R_BI, R_LAM, R_SC, R_SL) = (0, 1, 2, 3, 4, 8, 9, 10, 11, 12, 15)
NEG_DIST = 2.6e32


def need(eng, sem, value):
    if isinstance(value, int) and value <= 0:
        return
    eng.wait_ge(sem, value)


def hybrid_encoder(nc, A, out):
    DEPTH = A["w_in"].shape[0]
    with ExitStack() as ctx:
        base = (nc.sbuf_base + 31) // 32 * 32
        arena = {}

        def at(name, shape, dt, offset):
            size = 4
            for s in shape[1:]:
                size *= s
            assert offset + size <= nc.sbuf_usable_end, (name, offset + size)
            arena[name] = (offset, size)
            return nc.alloc_sbuf_tensor_at(name, shape, dt, offset=offset)

        top = [base]

        def room(nbytes):
            o = top[0]
            top[0] += (nbytes + 31) // 32 * 32
            assert top[0] <= nc.sbuf_usable_end, top[0] - nc.sbuf_usable_end
            return o

        def sb(name, shape, dt=F32):
            size = 4
            for s in shape[1:]:
                size *= s
            return at(name, shape, dt, room(size))

        def sem(name):
            return ctx.enter_context(nc.semaphore(name))

        TILE = NT * 4
        X = sb("X", [P, KT, NT])
        W_RAW_AT = room(WR * KT * P * 4)
        w_raw = at("w_raw", [P, WR, KT, P], F32, W_RAW_AT)
        w_lo = at("w_lo", [P, WR, KT, P], F32R, W_RAW_AT)
        w_hi = sb("w_hi", [P, 2, KT, P], F32R)
        ident = sb("ident", [P, P])
        ones = sb("ones", [P, P])
        dist_p = sb("dist_p", [P, NP_])
        dist_s = sb("dist_s", [NS, NKS])
        bias_p = sb("bias_p", [P, NP_])
        bias_s = sb("bias_s", [NS, NKS])
        par = sb("par", [P, KT, 32])
        half_b = sb("half_b", [P, 2, KT, 2])
        cs = sb("cs", [P, 2, KT])
        gs = sb("gs", [P, 2])
        neg_lam = sb("neg_lam", [P, 2])
        eps_col = sb("eps_col", [P, 1])
        rs_tok = sb("rs_tok", [P, 5])
        mx = sb("mx", [P, 2, 2])
        neg_mx = sb("neg_mx", [P, 2, 2])
        lsum = sb("lsum", [P, 2, 2])
        rl = sb("rl", [P, 2, 2])
        rl2 = sb("rl2", [P, 2])
        rs = sb("rs", [P, NT])
        last = sb("last", [P, 2, 8, KT])
        w_gate = sb("w_gate", [P, 2, 2, P])
        T = sb("T", [P, 2, NT])

        H_AT = room(2 * KT * TILE)
        h_hi = at("h_hi", [P, KT, NT], F32R, H_AT)
        h_lo = at("h_lo", [P, KT, NT], F32R, H_AT + KT * TILE)
        l_hi = at("l_hi", [P, KT, NT], F32R, H_AT)
        m_hi = at("m_hi", [P, KT, NT], F32R, H_AT + KT * TILE)
        BIG = room(4 * KT * TILE)
        O = at("O", [P, KT, NT], F32, BIG)
        o_lo = at("o_lo", [P, KT, NT], F32R, BIG)
        L = at("L", [P, KT, NT], F32, BIG + KT * TILE)
        l_lo = at("l_lo", [P, KT, NT], F32R, BIG + KT * TILE)
        GA = at("GA", [P, KT, NT], F32, BIG + 2 * KT * TILE)
        m_lo = at("m_lo", [P, KT, NT], F32R, BIG + 2 * KT * TILE)
        qk_hi = at("qk_hi", [P, 4, NT], F32R, BIG + 3 * KT * TILE)
        qk_lo = at("qk_lo", [P, 4, NT], F32R, BIG + 3 * KT * TILE + 4 * TILE)
        GB = at("GB", [P, KT, NT], F32, BIG + 3 * KT * TILE)
        u_hi = at("u_hi", [P, 16, NT], F32R, BIG)
        u_lo = at("u_lo", [P, 16, NT], F32R, BIG + 16 * TILE)
        V_AT = room(5 * 256 * 4 * 2 + 8192)
        v_hi = at("v_hi", [P, 5, 2, VD], F32R, V_AT)
        v_lo = at("v_lo", [P, 5, 2, VD], F32R, V_AT + 5120)
        pk_hi = at("pk_hi", [P, 2, PAST], F32R, V_AT + 10240)
        pk_lo = at("pk_lo", [P, 2, PAST], F32R, V_AT + 12288)
        pv_hi = at("pv_hi", [P, 2, 2 * VD], F32R, V_AT + 14336)
        pv_lo = at("pv_lo", [P, 2, 2 * VD], F32R, V_AT + 16384)
        o_hi = at("o_hi", [P, KT, NT], F32R, V_AT)
        Y = at("Y", [P, KT, NT], F32, V_AT)
        S_AT = room(14336)
        s1 = at("s1", [P, 3, 512], F32, S_AT)
        s2 = at("s2", [P, 2, 512], F32, S_AT + 6144)
        pt_hi = at("pt_hi", [P, 4, P], F32R, S_AT + 10240)
        pt_lo = at("pt_lo", [P, 4, P], F32R, S_AT + 12288)
        stage = at("stage", [P, 2, 5, P], F32, S_AT)
        sq_o = at("sq_o", [P, NT], F32, S_AT + 5120)
        rr = at("rr", [P, NT], F32, S_AT + 5120 + TILE)
        R_AT = room(7 * 552 * 4)
        U = at("U", [P, 2, 552], F32, R_AT)
        o_ = R_AT + 2 * 552 * 4
        uc, tr, aa, ti, tm = (at(n, [P, LW], F32, o_ + i * 552 * 4) for i, n in enumerate(["uc", "tr", "aa", "ti", "tm"]))
        pk_raw = at("pk_raw", [P, 2, 2, P], F32, o_ + 3 * 552 * 4)
        pv_raw = at("pv_raw", [P, 2, 2 * VD], F32, o_ + 4 * 552 * 4)
        acc_x = at("acc_x", [P, NT], F32, R_AT)
        acc_y = at("acc_y", [P, NT], F32, R_AT + TILE)
        sq = at("sq", [P, 2, NT], F32, R_AT + 2 * TILE)
        rn = at("rn", [P, NT], F32, R_AT + 4 * TILE)
        r2q = at("r2q", [P, NT], F32, R_AT + 5 * TILE)
        x_in = at("x_in", [P, 5, KT * P], F32, BIG)
        rows = at("rows", [32, KT * P], F32, BIG + 5 * 4096)
        lq = at("lq", [P, 2, 4, HD], F32, BIG + 6 * 4096)
        lprod = at("lprod", [P, HD], F32, BIG + 7 * 4096)
        lsc = at("lsc", [P, 8, KT * 2], F32, BIG + 7 * 4096 + 256)
        y_out = at("y_out", [P, 2, KT * P], F32, BIG)
        last_t = at("last_t", [P, P], F32, BIG + 8192)

        PJ = ctx.enter_context(nc.psum_tensor("PJ", [P, 2, 2, 512], F32))
        PX = ctx.enter_context(nc.psum_tensor("PX", [P, 4, 512], F32))

        w_landed = [sem(f"w_landed{i}") for i in range(WR)]
        w_hi_ready, w_lo_ready, tile_done, evacuated = map(sem, ("w_hi_ready", "w_lo_ready", "tile_done", "evacuated"))
        x_landed, par_landed, lam_landed = map(sem, ("x_landed", "par_landed", "lam_landed"))
        const_step, ident_ready = sem("const_step"), sem("ident_ready")
        norm_chain0, sp_step = sem("lambda_chain"), sem("param_chain")
        x_turned, x_placed, par_turned, par_step, lam_step, lam_act = map(
            sem, ("x_turned", "x_placed", "par_turned", "par_step", "lam_step", "lam_act"))
        h_hi_ready, h_lo_ready, x_squared, x_summed, x_ssq, x_rs = map(
            sem, ("h_hi_ready", "h_lo_ready", "x_squared", "x_summed", "x_ssq", "x_rs"))
        y_squared, y_summed, y_ssq, y_rs, y_scaled, x_new = map(
            sem, ("y_squared", "y_summed", "y_ssq", "y_rs", "y_scaled", "x_new"))
        rs_turned, rs_tok_ready = sem("rs_turned"), sem("rs_tok_ready")
        qk_hi_ready, qk_lo_ready, k_turned, k_staged = map(sem, ("qk_hi_ready", "qk_lo_ready", "k_turned", "k_staged"))
        v_hi_ready, v_lo_ready = sem("v_hi_ready"), sem("v_lo_ready")
        stored = [sem("stored0"), sem("stored1")]
        past_landed, past_turned, pk_hi_ready, pk_lo_ready, pv_hi_ready, pv_lo_ready = map(
            sem, ("past_landed", "past_turned", "pk_hi_ready", "pk_lo_ready", "pv_hi_ready", "pv_lo_ready"))
        bias_ready, scores_done, biased, max_ready, exp_done, norm_step, p_ready = map(
            sem, ("bias_ready", "scores_done", "biased", "max_ready", "exp_done", "norm_step", "p_ready"))
        p_turned, pt_hi_ready, pt_lo_ready, pv_done, o_placed = map(
            sem, ("p_turned", "pt_hi_ready", "pt_lo_ready", "pv_done", "o_placed"))
        o_squared, o_ssq, o_rs, o_normed, o_hi_ready, o_lo_ready = map(
            sem, ("o_squared", "o_ssq", "o_rs", "o_normed", "o_hi_ready", "o_lo_ready"))
        wg_zero, wg_landed, hist_ready, conv_first, conv_step, gates_done, lru_act, lru_step = map(
            sem, ("wg_zero", "wg_landed", "hist_ready", "conv_first", "conv_step", "gates_done", "lru_act", "lru_step"))
        gelu_done, ga_done, gb_done, l_hi_ready, l_lo_ready, b_scaled, m_hi_ready, m_lo_ready = map(
            sem, ("gelu_done", "ga_done", "gb_done", "l_hi_ready", "l_lo_ready", "b_scaled", "m_hi_ready", "m_lo_ready"))
        relu2_done, u_hi_ready, u_lo_ready, f_scaled = map(sem, ("relu2_done", "u_hi_ready", "u_lo_ready", "f_scaled"))
        out_turned, out_placed, last_turned, last_placed = map(sem, ("out_turned", "out_placed", "last_turned", "last_placed"))
        out_stored = [sem("out_stored0"), sem("out_stored1")]
        last_stored = sem("last_stored")

        def halves(t):
            return t.rearrange("p (a b) -> p a b", a=2)

        def cols(g):
            return slice(0, P) if g == 0 else slice(NS + P * (g - 1), NS + P * g)

        def proj(n):
            return PJ[:, n % 2, :, 0:HT]

        def gain(l, k, row):
            return par[:, k, 16 * l + row:16 * l + row + 1]

        def weight_source(l, i):
            if i < T_GB:
                p, j = i // 12, i % 12
                first = [0, 512, 1024, 1536][j] + P * p if j < 4 else [2048, 3072, 4096, 5120][(j - 4) // 2] + 256 * p + P * (j % 2)
                w, r0 = A["w_in"], 0
            elif i < T_WA:
                w, r0, first = A["w_in"], 0, 6144 + P * (i - T_GB)
            elif i < T_WL:
                w, r0, first = A["w_branch_attn"], 0, P * (i - T_WA)
            elif i < T_WO:
                w, r0, first = A["w_branch_lru"], 0, P * (i - T_WL)
            elif i < T_MLP:
                w, r0, first = A["w_out"], 0, P * (i - T_WO)
            else:
                c, j = (i - T_MLP) // 32, (i - T_MLP) % 32
                if j < 16:
                    w, r0, first = A["w_up"], 0, c * 2048 + P * j
                else:
                    w, r0, first = A["w_down"], c * 2048 + 1024 * (j % 2), P * ((j - 16) // 2)
            return w[l, r0:r0 + KT * P, first:first + P].rearrange("(k p) n -> p k n", p=P)

        o_turns = [(), (0, 1), (2, 3), (4,), (5,), (6,), (7,), ()]

        block = ctx.enter_context(nc.Block())

        @block.sync
        def _(sp):
            sp.dma_start(x_in[0:NS, 0, :], A["x_sample"][0]).then_inc(x_landed, 16)
            sp.dma_start(x_in[:, 1:5, :], A["x_prompt"][0].rearrange("(g t) d -> t g d", t=P)).then_inc(x_landed, 16)
            for l in range(DEPTH):
                r = rows[16 * l:16 * l + 16, :]
                for row, name in ((R_GPRE, "g_mix_pre"), (R_GPOST, "g_mix_post"), (R_MPRE, "g_mlp_pre"), (R_MPOST, "g_mlp_post"),
                                  (R_CB, "conv_b"), (R_BR, "b_rg"), (R_BI, "b_ig"), (R_LAM, "lru_lambda")):
                    sp.dma_start(r[row:row + 1, :], A[name][l:l + 1]).then_inc(par_landed, 16)
                sp.dma_start(r[R_CW:R_CW + 4, :], A["conv_w"][l]).then_inc(par_landed, 16)
                sp.dma_start(r[R_SC:R_SC + 3, :], A["state_conv"][l, 0]).then_inc(par_landed, 16)
                sp.dma_start(r[R_SL:R_SL + 1, :], A["state_lru"][l]).then_inc(par_landed, 16)
            for l in range(DEPTH):
                for i in range(TL):
                    n = TL * l + i
                    need(sp, tile_done, n - WR + 1)
                    sp.dma_start(w_raw[:, n % WR, :, :], weight_source(l, i)).then_inc(w_landed[n % WR], 16)

        PAR_DMAS = 11 * DEPTH

        @block.gpsimd
        def _(pool):
            pool.memset(ident[:], 0.0).then_inc(const_step, 1)
            pool.wait_ge(const_step, 1)
            pool.affine_select(out=ident[:], in_=ident[:], compare_op=ALU.not_equal, fill=1.0, base=0,
                               pattern=[[-1, P]], channel_multiplier=1).then_inc(ident_ready, 1)
            pool.iota(dist_p[:], [[-1, NP_]], base=NP_ - P, channel_multiplier=1,
                      allow_small_or_imprecise_dtypes=True).then_inc(const_step, 1)
            pool.iota(dist_s[:], [[-1, NKS]], base=PAST, channel_multiplier=1,
                      allow_small_or_imprecise_dtypes=True).then_inc(const_step, 1)
            pool.memset(w_gate[:], 0.0).then_inc(wg_zero, 1)
            for l in range(DEPTH):
                for j, name in enumerate(("lambda_q1", "lambda_k1", "lambda_q2", "lambda_k2")):
                    pool.dma_start(lq[:, l, j, :], A[name][l].partition_broadcast(P)).then_inc(lam_landed, 16)
                with nc.allow_non_contiguous_dma(reason="128 values"):
                    pool.dma_start(gs[:, l:l + 1], A["g_sub"][l].rearrange("(p o) -> p o", o=1)).then_inc(lam_landed, 16)

            def load_gate_weights(l, p):
                g = 4 * l + p
                need(pool, wg_zero, 1)
                need(pool, gates_done, 2 * g)
                for u in range(2):
                    for j, name in enumerate(("w_rg", "w_ig")):
                        for b in range(2):
                            pool.dma_start(w_gate[64 * b:64 * b + 64, u, j, 64 * b:64 * b + 64],
                                           A[name][l, 4 * p + 2 * u + b]).then_inc(wg_landed, 16)

            def load_past(l, p):
                g = 4 * l + p
                need(pool, past_turned, g)
                need(pool, pv_lo_ready, g)
                if p > 0:
                    need(pool, lru_step, 24 * (g - 1))
                else:
                    need(pool, f_scaled, 8 * l)
                for m in range(2):
                    pool.dma_start(pk_raw[:, :, m, :], A["cache_k"][l, 0].rearrange("(a t) (m h) d -> m t a (h d)", t=P, m=2)[m][
                        :, :, P * p:P * p + P]).then_inc(past_landed, 16)
                pool.dma_start(pv_raw[:], A["cache_v"][l, 0].rearrange("(a t) h d -> t a (h d)", t=P)[
                    :, :, 256 * p:256 * p + 256]).then_inc(past_landed, 16)

            def past_lo(g):
                pool.wait_ge(pv_hi_ready, g + 1)
                pool.tensor_tensor(pv_lo[:], pv_raw[:], pv_hi[:].bitcast(F32), ALU.subtract).then_inc(pv_lo_ready, 1)

            def store_rows(l, p, j):
                g = 4 * l + p
                if j < 2:
                    pool.wait_ge(k_staged, 2 * g + j + 1)
                    c = 512 * j + P * p
                    to_p = out["prompt_k"][l, 0].rearrange("(g t) h d -> t g (h d)", t=P)[:, :, c:c + P]
                    to_s = out["sample_k"][l, 0].rearrange("t h d -> t (h d)")[:, c:c + P]
                else:
                    pool.wait_ge(evacuated, TL * l + 12 * p + 2 + j + 1)
                    h = 2 * p + j - 2
                    to_p = out["prompt_v"][l, 0].rearrange("(g t) h d -> t g (h d)", t=P)[:, :, VD * h:VD * h + VD]
                    to_s = out["sample_v"][l, 0].rearrange("t h d -> t (h d)")[:, VD * h:VD * h + VD]
                pool.dma_start(to_p, stage[:, j % 2, 1:5, :]).then_inc(stored[j % 2], 16)
                pool.dma_start(to_s, stage[0:NS, j % 2, 0, :]).then_inc(stored[j % 2], 16)

            for l in range(DEPTH):
                for p in range(4):
                    g = 4 * l + p
                    if p == 0:
                        load_past(l, 0)
                    else:
                        past_lo(g)
                    for i in range(4):
                        pool.wait_ge(qk_hi_ready, 4 * g + i + 1)
                        pool.tensor_tensor(qk_lo[:, i, :], T[:, i % 2, :], qk_hi[:, i, :].bitcast(F32), ALU.subtract).then_inc(qk_lo_ready, 1)
                        if i >= 2:
                            store_rows(l, p, i - 2)
                    if p == 0:
                        past_lo(g)
                    for u in range(2):
                        store_rows(l, p, 2 + u)
                        pool.wait_ge(v_hi_ready, 2 * g + u + 1)
                        pool.tensor_tensor(v_lo[:, :, u, :], stage[:, u, :, :], v_hi[:, :, u, :].bitcast(F32), ALU.subtract).then_inc(v_lo_ready, 1)
                    if p < 3:
                        load_past(l, p + 1)
                    load_gate_weights(l, p)
                for i in range(KT):
                    pool.wait_ge(m_hi_ready, KT * l + i + 1)
                    pool.tensor_tensor(m_lo[:, i, :], GB[:, i, :], m_hi[:, i, :].bitcast(F32), ALU.subtract).then_inc(m_lo_ready, 1)
                for c in range(2):
                    for i in range(16):
                        pool.wait_ge(u_hi_ready, 32 * l + 16 * c + i + 1)
                        pool.tensor_tensor(u_lo[:, i, :], T[:, i % 2, :], u_hi[:, i, :].bitcast(F32), ALU.subtract).then_inc(u_lo_ready, 1)
            pool.wait_ge(stored[0], 32 * 2 * 4 * DEPTH)
            pool.wait_ge(stored[1], 32 * 2 * 4 * DEPTH)
            pool.wait_ge(last_placed, 1)
            for l in range(DEPTH):
                for r, name, n in ((0, "prompt_conv", 3), (3, "sample_conv", 3), (6, "prompt_lru", 1), (7, "sample_lru", 1)):
                    q = (l * 8 + r) * KT
                    dst = out[name][l, 0].rearrange("r (k c) -> (r k) c", c=P) if n == 3 else out[name][l, 0].rearrange("(k c) -> k c", c=P)
                    pool.dma_start(dst, last_t[q:q + n * KT, :]).then_inc(last_stored, 16)
            for g in range(5):
                pool.wait_ge(out_placed, g + 1)
                if g == 0:
                    pool.dma_start(out["y_sample"][0], y_out[0:NS, 0, :]).then_inc(out_stored[0], 16)
                else:
                    pool.dma_start(out["y_prompt"][0, P * (g - 1):P * g, :], y_out[:, g % 2, :]).then_inc(out_stored[g % 2], 16)
            pool.wait_ge(last_stored, 16 * 4 * DEPTH)
            pool.wait_ge(out_stored[0], 48)
            pool.wait_ge(out_stored[1], 32)

        @block.tensor
        def _(pe):
            def split_product(ps, w, x, start, stop, mms):
                for a, b in ((0, 0), (0, 1), (1, 0)):
                    for o, c in mms:
                        mm = pe.matmul(o, w[a], x[b][c], start=start and a + b == 0, stop=stop and a == 1)
                return mm

            def tile_in(n):
                pe.wait_ge(w_lo_ready, n + 1)

            def gemm(n, src, k0, buf, free, first=True, end=True, ks=range(KT), waits=None):
                if ks[0] == 0:
                    tile_in(n)
                    need(pe, evacuated, free)
                for k in ks:
                    if waits is not None:
                        pe.wait_ge(waits[0], waits[1] + k)
                    w = (w_hi[:, n % 2, k, :], w_lo[:, n % WR, k, :])
                    for a, b in ((0, 0), (0, 1), (1, 0)):
                        for half in range(2):
                            mm = pe.matmul(PJ[:, buf, half, 0:HT], w[a], src[b][:, k0 + k, HT * half:HT * half + HT],
                                           start=first and k == 0 and a + b == 0, stop=end and k == KT - 1 and a == 1)
                if ks[-1] == KT - 1:
                    mm.then_inc(tile_done, 1)

            H = (h_hi, h_lo)

            def gemm_pair(n, free, waits):
                tile_in(n)
                tile_in(n + 1)
                need(pe, evacuated, free)
                for k in range(KT):
                    pe.wait_ge(waits[0], waits[1] + k)
                    for m in (n, n + 1):
                        w = (w_hi[:, m % 2, k, :], w_lo[:, m % WR, k, :])
                        for a, b in ((0, 0), (0, 1), (1, 0)):
                            for half in range(2):
                                mm = pe.matmul(PJ[:, m % 2, half, 0:HT], w[a], H[b][:, k, HT * half:HT * half + HT],
                                               start=k == 0 and a + b == 0, stop=k == KT - 1 and a == 1)
                        if k == KT - 1:
                            mm.then_inc(tile_done, 1)

            def ones_sum(src, bank=0):
                for half in range(2):
                    mm = pe.matmul(PX[:, bank + half, 0:HT], ones[:], src[:, HT * half:HT * half + HT], start=True, stop=True)
                return mm

            def gates(l, p, u):
                g2 = 2 * (4 * l + p) + u
                pe.wait_ge(wg_landed, 16 * 8 * (4 * l + p + 1))
                pe.wait_ge(conv_step, 3 * g2 + 3)
                need(pe, lru_act, 5 * g2)
                for j in range(2):
                    for half in range(2):
                        mm = pe.matmul(PX[:, 2 * j + half, 0:LH], w_gate[:, u, j, :], uc[:, LH * half:LH * half + LH], start=True, stop=True)
                mm.then_inc(gates_done, 1)

            def sub_ssq(l, p, u):
                g2 = 2 * (4 * l + p) + u
                pe.wait_ge(o_squared, g2 + 1)
                pe.wait_ge(lru_act, 5 * g2 + 2)
                ones_sum(sq_o, 2).then_inc(o_ssq, 1)

            def turn_k(l, p, m):
                g = 4 * l + p
                n = TL * l + 12 * p + 2 + m
                pe.wait_ge(evacuated, n + 1)
                need(pe, k_staged, 2 * g + m)
                if p > 0:
                    pe.wait_ge(lru_act, 10 * g - 9 + 5 * m)
                for grp in range(5):
                    o = PX[:, 1, 0:P] if grp == 0 else PX[:, 0, P * (grp - 1):P * grp]
                    mm = pe.transpose(o, T[:, m % 2, cols(grp)], ident[:])
                mm.then_inc(k_turned, 1)

            def turn_past(l, p):
                g = 4 * l + p
                pe.wait_ge(past_landed, 48 * (g + 1))
                need(pe, pt_lo_ready, 10 * g)
                for m in range(2):
                    for a in range(2):
                        mm = pe.transpose(PX[:, 2, 256 * m + P * a:256 * m + P * a + P], pk_raw[:, a, m, :], ident[:])
                mm.then_inc(past_turned, 1)

            def v_tile(l, p, u):
                n = TL * l + 12 * p + 4 + u
                tile_in(n)
                need(pe, evacuated, n - 1)
                for grp in range(5):
                    o = PJ[:, n % 2, 1, 0:P] if grp == 0 else PJ[:, n % 2, 0, P * (grp - 1):P * grp]
                    for k in range(KT):
                        w = (w_hi[:, n % 2, k, :], w_lo[:, n % WR, k, :])
                        for a, b in ((0, 0), (0, 1), (1, 0)):
                            mm = pe.matmul(o, H[a][:, k, cols(grp)], w[b], start=k == 0 and a + b == 0, stop=k == KT - 1 and a == 1)
                mm.then_inc(tile_done, 1)

            def scores(l, p, s):
                g = 4 * l + p
                sg, u, qs = 10 * g + s, s // 5, s % 5
                r = slice(HD * u, HD * u + HD)
                if s == 0:
                    pe.wait_ge(qk_lo_ready, 4 * g + 4)
                    pe.wait_ge(pk_lo_ready, g + 1)
                    pe.wait_ge(k_staged, 2 * g + 2)
                need(pe, biased, 2 * sg)
                QK = (qk_hi, qk_lo)
                PK = (pk_hi, pk_lo)
                for m in range(2):
                    if qs == 0:
                        for a, b in ((0, 0), (0, 1), (1, 0)):
                            pe.matmul(PX[:, m, 0:PAST], QK[a][r, m, 0:P], PK[b][r, m, :], start=a + b == 0, stop=a == 1)
                        for a, b in ((0, 0), (0, 1), (1, 0)):
                            mm = pe.matmul(PX[:, m, PAST:NKS], QK[a][r, m, 0:P], QK[b][r, 2 + m, 0:NS], start=a + b == 0, stop=a == 1)
                    else:
                        kw = P * qs
                        for a, b in ((0, 0), (0, 1), (1, 0)):
                            mm = pe.matmul(PX[:, m, 0:kw], QK[a][r, m, cols(qs)], QK[b][r, 2 + m, NS:NS + kw], start=a + b == 0, stop=a == 1)
                mm.then_inc(scores_done, 1)

            def turn_p(l, p, s):
                sg, u, qs = 10 * (4 * l + p) + s, s // 5, s % 5
                pe.wait_ge(p_ready, sg + 1)
                need(pe, pt_lo_ready, sg)
                if s == 0 and p > 0:
                    pe.wait_ge(o_rs, 4 * g - 1)
                src = s1[:, s % 3, :]
                if qs == 0:
                    for kt in range(3):
                        mm = pe.transpose(PX[:, 2, P * kt:P * kt + NS], src[0:NS, P * kt:P * kt + P], ident[0:NS, 0:NS])
                else:
                    for kt in range(qs):
                        mm = pe.transpose(PX[:, 2, P * kt:P * kt + P], src[:, P * kt:P * kt + P], ident[:])
                mm.then_inc(p_turned, 1)

            def weigh_v(l, p, s):
                g = 4 * l + p
                sg, u, qs = 10 * g + s, s // 5, s % 5
                if s == 0:
                    pe.wait_ge(v_lo_ready, 2 * g + 2)
                    pe.wait_ge(pv_lo_ready, g + 1)
                pe.wait_ge(pt_lo_ready, sg + 1)
                need(pe, o_placed, sg)
                V, PV, PT = (v_hi, v_lo), (pv_hi, pv_lo), (pt_hi, pt_lo)
                kts = range(3) if qs == 0 else range(qs)
                w = NS if qs == 0 else P
                for kt in kts:
                    for a, b in ((0, 0), (0, 1), (1, 0)):
                        if qs > 0:
                            v, pt = V[a][:, 1 + kt, u, :], PT[b][:, kt, :]
                        elif kt < 2:
                            v, pt = PV[a][:, kt, VD * u:VD * u + VD], PT[b][:, kt, 0:NS]
                        else:
                            v, pt = V[a][0:NS, 0, u, :], PT[b][0:NS, 2, 0:NS]
                        mm = pe.matmul(PX[:, 3, 0:w], v, pt, start=kt == 0 and a + b == 0, stop=kt == kts[-1] and a == 1)
                mm.then_inc(pv_done, 1)

            pe.wait_ge(ident_ready, 1)
            pe.wait_ge(par_landed, 16 * PAR_DMAS)
            for k in range(KT):
                mm = pe.transpose(PX[:, 0, 32 * k:32 * k + 32], rows[0:32, P * k:P * k + P], ident[0:32, 0:32])
            mm.then_inc(par_turned, 1)
            pe.wait_ge(x_landed, 32)
            for k in range(KT):
                need(pe, x_placed, k - 1)
                for grp in range(5):
                    if grp == 0:
                        o = PJ[:, k % 2, 0, 0:NS]
                    else:
                        o = PJ[:, k % 2, (grp - 1) // 2, (NS if grp < 3 else 0) + P * ((grp - 1) % 2):][:, 0:P]
                    if grp == 0:
                        mm = pe.transpose(o, x_in[0:NS, 0, P * k:P * k + P], ident[0:NS, 0:NS])
                    else:
                        mm = pe.transpose(o, x_in[:, grp, P * k:P * k + P], ident[:])
                mm.then_inc(x_turned, 1)
            pe.wait_ge(x_placed, KT)

            for l in range(DEPTH):
                N = TL * l
                for p in range(4):
                    g, n = 4 * l + p, N + 12 * p
                    if p == 0:
                        gemm_pair(n, n, (h_lo_ready, 8 * 2 * l + 1))
                        pe.wait_ge(x_summed, 7 * 2 * l + 7)
                        need(pe, y_rs, 4 * l)
                        ones_sum(acc_x).then_inc(x_ssq, 1)
                        pe.wait_ge(x_rs, 4 * l + 2)
                        for grp in range(5):
                            mm = pe.matmul(PX[:, 3, 2 * grp:2 * grp + 2], rs[:, cols(grp)], ident[:, 0:2], start=True, stop=True)
                        mm.then_inc(rs_turned, 1)
                    else:
                        gemm(n, H, 0, 0, n - 1)
                        weigh_v(l, p - 1, 9)
                        turn_past(l, p)
                        gemm(n + 1, H, 0, 1, n)
                        pe.wait_ge(pk_lo_ready, g + 1)
                        gates(l, p - 1, 0)
                    gemm(n + 2, H, 0, 0, n + 1)
                    if p > 0:
                        sub_ssq(l, p - 1, 0)
                    gemm(n + 3, H, 0, 1, n + 2, ks=range(0, 4))
                    turn_k(l, p, 0)
                    gemm(n + 3, H, 0, 1, n + 2, ks=range(4, 8))
                    if p > 0:
                        pe.wait_ge(o_rs, 4 * g - 3)
                        pe.wait_ge(k_staged, 2 * g + 1)
                        gates(l, p - 1, 1)
                    v_tile(l, p, 0)
                    turn_k(l, p, 1)
                    if p == 0:
                        turn_past(l, p)
                    else:
                        sub_ssq(l, p - 1, 1)
                    v_tile(l, p, 1)
                    for j in range(12):
                        i = n + 6 + j // 2
                        gemm(i, H, 0, i % 2, i - 1, ks=range(4 * (j % 2), 4 * (j % 2) + 4))
                        if j >= 3:
                            weigh_v(l, p, j - 3)
                        if j < 10:
                            scores(l, p, j)
                        if j >= 2:
                            turn_p(l, p, j - 2)
                g = 4 * l + 3
                for i in range(8):
                    n = N + T_GB + i
                    gemm(n, H, 0, n % 2, n - 1)
                    if i == 0:
                        weigh_v(l, 3, 9)
                        pe.wait_ge(o_placed, 10 * (g + 1))
                    if i in (1, 3):
                        if i == 3:
                            pe.wait_ge(o_rs, 2 * (2 * g) + 1)
                        gates(l, 3, i // 2)
                    if i in (2, 4):
                        sub_ssq(l, 3, i // 2 - 1)
                for i in range(8):
                    n = N + T_WA + i
                    gemm(n, (o_hi, o_lo), 0, n % 2, n - 1, waits=(o_lo_ready, 8 * l + 1) if i == 0 else None)
                for i in range(8):
                    n = N + T_WL + i
                    if i == 0:
                        pe.wait_ge(l_lo_ready, 8 * (l + 1))
                    gemm(n, (l_hi, l_lo), 0, n % 2, n - 1)
                for i in range(8):
                    n = N + T_WO + i
                    gemm(n, (m_hi, m_lo), 0, n % 2, n - 1, waits=(m_lo_ready, 8 * l + 1) if i == 0 else None)
                pe.wait_ge(y_summed, 7 * 2 * l + 7)
                ones_sum(acc_y).then_inc(y_ssq, 1)
                for c in range(2):
                    for i in range(16):
                        n = N + T_MLP + 32 * c + i
                        if c == 0 and i == 0:
                            gemm_pair(n, n, (h_lo_ready, 8 * (2 * l + 1) + 1))
                        elif c == 1 or i > 1:
                            gemm(n, H, 0, n % 2, n - 2 if i == 0 else n - 1)
                        if c == 0 and i == 1:
                            pe.wait_ge(x_summed, 7 * (2 * l + 1) + 7)
                            pe.wait_ge(y_rs, 4 * l + 2)
                            ones_sum(acc_x).then_inc(x_ssq, 1)
                    for m in range(8):
                        n = N + T_MLP + 32 * c + 16 + 2 * m
                        for half in range(2):
                            gemm(n + half, (u_hi, u_lo), 8 * half, m % 2, (n - 1 if m == 0 else n - 2) if half == 0 else 0,
                                 first=half == 0, end=half == 1,
                                 waits=(u_lo_ready, 16 * (2 * l + c) + 8 * half + 1) if m == 0 else None)
                pe.wait_ge(y_summed, 7 * (2 * l + 1) + 7)
                pe.wait_ge(x_rs, 4 * l + 4)
                ones_sum(acc_y).then_inc(y_ssq, 1)
            pe.wait_ge(lru_step, 12 * 8 * DEPTH)
            pe.wait_ge(y_rs, 4 * DEPTH)
            pe.transpose(PX[:, 0, 0:P], last[:].rearrange("p l r k -> p (l r k)"), ident[:]).then_inc(last_turned, 1)
            pe.wait_ge(x_new, 8 * 2 * DEPTH)
            for grp in range(5):
                need(pe, out_placed, grp - 1) if grp > 1 else need(pe, evacuated, TL * DEPTH)
                for k in range(KT):
                    mm = pe.transpose(PJ[:, grp % 2, k // 4, P * (k % 4):P * (k % 4) + P], X[:, k, cols(grp)], ident[:])
                mm.then_inc(out_turned, 1)

        @block.scalar
        def _(act):
            def split_hi(n):
                act.wait_ge(w_landed[n % WR], 16 * (n // WR + 1))
                need(act, tile_done, n - 1)
                act.activation(w_hi[:, n % 2, :, :], w_raw[:, n % WR, :, :], ACT.Copy).then_inc(w_hi_ready, 1)

            def input_tile(l, s, k):
                S = 2 * l + s
                if S == 0:
                    act.wait_ge(x_placed, k + 1)
                    act.wait_ge(par_step, 1)
                else:
                    act.wait_ge(x_new, 8 * (S - 1) + k + 1)
                act.activation(h_hi[:, k, :], X[:, k, :], ACT.Copy, scale=gain(l, k, R_MPRE if s else R_GPRE)).then_inc(h_hi_ready, 1)

            def x_square(l, s, k):
                S = 2 * l + s
                if k == 0:
                    need(act, x_ssq, S)
                    act.activation(acc_x[:], X[:, k, :], ACT.Square).then_inc(x_squared, 1)
                else:
                    if k > 2:
                        act.wait_ge(x_summed, 7 * S + k - 2)
                    act.activation(sq[:, k % 2, :], X[:, k, :], ACT.Square).then_inc(x_squared, 1)

            def y_square(l, s, k):
                Y_ = 2 * l + s
                if k == 0:
                    need(act, y_ssq, Y_)
                    act.activation(acc_y[:], Y[:, k, :], ACT.Square).then_inc(y_squared, 1)
                else:
                    if k > 2:
                        act.wait_ge(y_summed, 7 * Y_ + k - 2)
                    act.activation(sq[:, k % 2, :], Y[:, k, :], ACT.Square).then_inc(y_squared, 1)

            def inverse_rms(dst, ssq, value, done, count, power):
                act.wait_ge(ssq, value)
                act.activation(halves(dst), PX[:, 0:2, 0:HT], ACT.Ln, scale=1.0 / (KT * P), bias=eps_col[:, 0:1]).then_inc(done, 1)
                act.wait_ge(done, count + 1)
                act.activation(dst, dst, ACT.Exp, scale=power).then_inc(done, 1)

            def qk_split(l, p, i):
                g = 4 * l + p
                act.wait_ge(evacuated, TL * l + 12 * p + i + 1)
                act.activation(qk_hi[:, i, :], T[:, i % 2, :], ACT.Copy).then_inc(qk_hi_ready, 1)

            def stage_k(l, p, m):
                g = 4 * l + p
                act.wait_ge(k_turned, 2 * g + m + 1)
                need(act, stored[m], 32 * 2 * g)
                if g > 0 and m == 0:
                    act.wait_ge(pv_done, 10 * g)
                act.activation(stage[0:NS, m, 0, :], PX[0:NS, 1, 0:P], ACT.Copy)
                act.activation(stage[:, m, 1:5, :], PX[:, 0, :].rearrange("p (g c) -> p g c", c=P), ACT.Copy).then_inc(k_staged, 1)

            def v_split(l, p, u):
                g = 4 * l + p
                act.wait_ge(evacuated, TL * l + 12 * p + 4 + u + 1)
                act.activation(v_hi[:, :, u, :], stage[:, u, :, :], ACT.Copy).then_inc(v_hi_ready, 1)

            def past_split(l, p):
                g = 4 * l + p
                act.wait_ge(past_turned, g + 1)
                act.activation(pk_hi[:], PX[:, 2, :].rearrange("p (m c) -> p m c", m=2), ACT.Copy).then_inc(pk_hi_ready, 1)
                act.activation(pv_hi[:], pv_raw[:], ACT.Copy).then_inc(pv_hi_ready, 1)

            def exponents(l, p, s):
                sg, qs = 10 * (4 * l + p) + s, s % 5
                nr, w, b = (NS, NKS, s % 2) if qs == 0 else (P, P * qs, s % 2)
                act.wait_ge(max_ready, sg + 1)
                for m in range(2):
                    buf = s1[0:nr, s % 3, 0:w] if m == 0 else s2[0:nr, b, 0:w]
                    act.activation(buf, buf, ACT.Exp, bias=neg_mx[0:nr, b, m:m + 1], scale=SCALE,
                                   accum_out=lsum[0:nr, b, m:m + 1]).then_inc(exp_done, 1)

            def p_split(l, p, s):
                sg, qs = 10 * (4 * l + p) + s, s % 5
                act.wait_ge(p_turned, sg + 1)
                need(act, pv_done, sg)
                nk, w = (3, NS) if qs == 0 else (qs, P)
                act.activation(pt_hi[:, 0:nk, 0:w], PX[:, 2, 0:P * nk].rearrange("p (k c) -> p k c", c=P)[:, :, 0:w], ACT.Copy).then_inc(pt_hi_ready, 1)

            def place_o(l, p, s):
                sg, u, qs = 10 * (4 * l + p) + s, s // 5, s % 5
                act.wait_ge(pv_done, sg + 1)
                w, c = (NS, slice(0, NS)) if qs == 0 else (P, cols(qs))
                act.activation(O[:, 2 * p + u, c], PX[:, 3, 0:w], ACT.Copy).then_inc(o_placed, 1)

            def gelu(l, p, u):
                act.wait_ge(evacuated, TL * l + 12 * p + 8 + u + 1)
                act.activation(L[:, 2 * p + u, :], T[:, u, :], ACT.Gelu_apprx_tanh).then_inc(gelu_done, 1)

            def gate_a(l, p, u):
                act.wait_ge(evacuated, TL * l + 12 * p + 10 + u + 1)
                act.activation(GA[:, 2 * p + u, :], T[:, u, :], ACT.Tanh, scale=0.5).then_inc(ga_done, 1)

            def conv_start(l, p, u):
                g2 = 2 * (4 * l + p) + u
                f = 2 * p + u
                act.wait_ge(evacuated, TL * l + 12 * p + 6 + u + 1)
                need(act, lru_step, 12 * (g2 - 1) + 3 if g2 else 0)
                act.activation(uc[:], U[:, u, 0:LW], ACT.Identity, scale=gain(l, f, R_CW), bias=gain(l, f, R_CB)).then_inc(conv_first, 1)

            def gate_acts(l, p, u):
                g2 = 2 * (4 * l + p) + u
                f = 2 * p + u
                act.wait_ge(gates_done, g2 + 1)
                need(act, lru_step, 12 * g2)
                need(act, pv_lo_ready, 4 * l + p + 2 if p < 3 else 0)
                for j, t in enumerate((tr, ti)):
                    act.activation(t[:].rearrange("p (a b) -> p a b", a=2), PX[:, 2 * j:2 * j + 2, 0:LH], ACT.Tanh, scale=0.5,
                                   bias=half_b[:, l, f, j:j + 1]).then_inc(lru_act, 1)
                act.wait_ge(lru_act, 5 * g2 + 1)
                act.activation(aa[:], tr[:], ACT.Exp, scale=cs[:, l, f:f + 1], bias=cs[:, l, f:f + 1]).then_inc(lru_act, 1)
                act.wait_ge(lru_act, 5 * g2 + 3)
                act.activation(tr[:], tr[:], ACT.Tanh, scale=cs[:, l, f:f + 1], bias=cs[:, l, f:f + 1]).then_inc(lru_act, 1)

            def lru_root(l, p, u):
                g2 = 2 * (4 * l + p) + u
                act.wait_ge(lru_step, 12 * g2 + 2)
                act.activation(tm[:], tm[:], ACT.Sqrt, scale=-1.0).then_inc(lru_act, 1)

            def sub_square(l, p, u):
                g2 = 2 * (4 * l + p) + u
                act.wait_ge(o_placed, 10 * (4 * l + p) + 5 * u + 5)
                act.wait_ge(pv_done, 10 * (4 * l + p) + 10)
                need(act, o_ssq, g2)
                act.activation(sq_o[:], O[:, 2 * p + u, :], ACT.Square).then_inc(o_squared, 1)

            def sub_rs(l, p, u):
                g2 = 2 * (4 * l + p) + u
                act.wait_ge(o_ssq, g2 + 1)
                need(act, o_normed, g2)
                act.activation(halves(rr[:]), PX[:, 2:4, 0:HT], ACT.Ln, scale=1.0 / VD, bias=eps_col[:, 0:1]).then_inc(o_rs, 1)
                act.wait_ge(o_rs, 2 * g2 + 1)
                act.activation(rr[:], rr[:], ACT.Exp, scale=-0.5).then_inc(o_rs, 1)

            act.wait_ge(par_step, 2)
            act.activation(lsc[:, 1, :], lsc[:, 0, :], ACT.Exp, scale=-1.0).then_inc(lam_act, 1)
            act.wait_ge(lam_step, 4)
            act.activation(lsc[:, 7, 0:4], lsc[:, 6, 0:4], ACT.Exp).then_inc(lam_act, 1)
            split_hi(0)
            split_hi(1)
            for k in range(KT):
                input_tile(0, 0, k)
            for k in range(KT):
                x_square(0, 0, k)

            for l in range(DEPTH):
                N = TL * l
                for p in range(4):
                    n = N + 12 * p
                    for i in range(6):
                        if not (p == 0 and i == 0):
                            split_hi(n + i + 1)
                        if p == 0 and i == 0:
                            inverse_rms(rs[:], x_ssq, 2 * l + 1, x_rs, 4 * l, -0.5)
                        if i == 2 and p > 0:
                            gate_acts(l, p - 1, 0)
                            conv_start(l, p - 1, 1)
                            lru_root(l, p - 1, 0)
                        if i == 3 and p > 0:
                            sub_rs(l, p - 1, 0)
                        if i == 3:
                            stage_k(l, p, 0)
                        if i < 4:
                            qk_split(l, p, i)
                        if i == 0 and p > 0:
                            place_o(l, p - 1, 9)
                            past_split(l, p)
                            sub_square(l, p - 1, 0)
                        if i == 3 and p > 0:
                            sub_square(l, p - 1, 1)
                        if i == 4:
                            if p > 0:
                                gate_acts(l, p - 1, 1)
                                lru_root(l, p - 1, 1)
                            v_split(l, p, 0)
                            stage_k(l, p, 1)
                            if p == 0:
                                past_split(l, p)
                        if i == 5:
                            if p > 0:
                                sub_rs(l, p - 1, 1)
                            v_split(l, p, 1)
                    for j in range(12):
                        if j % 2 == 0:
                            split_hi(n + 7 + j // 2)
                        if 3 <= j:
                            place_o(l, p, j - 3)
                        if 2 <= j:
                            p_split(l, p, j - 2)
                        if j < 10:
                            exponents(l, p, j)
                        if j == 7:
                            gelu(l, p, 0)
                            gelu(l, p, 1)
                        if j in (9, 11):
                            gate_a(l, p, (j - 9) // 2)
                        if j == 6:
                            conv_start(l, p, 0)
                for i in range(8):
                    n = N + T_GB + i
                    split_hi(n + 1)
                    act.wait_ge(evacuated, n + 1)
                    act.activation(GB[:, i, :], T[:, i % 2, :], ACT.Tanh, scale=0.5).then_inc(gb_done, 1)
                    if i == 0:
                        place_o(l, 3, 9)
                        sub_square(l, 3, 0)
                    if i == 1:
                        gate_acts(l, 3, 0)
                        conv_start(l, 3, 1)
                        lru_root(l, 3, 0)
                    if i == 2:
                        sub_rs(l, 3, 0)
                        sub_square(l, 3, 1)
                    if i == 3:
                        gate_acts(l, 3, 1)
                        lru_root(l, 3, 1)
                    if i == 4:
                        sub_rs(l, 3, 1)
                    for f in o_turns[i]:
                        act.wait_ge(o_normed, 8 * l + f + 1)
                        act.activation(o_hi[:, f, :], O[:, f, :], ACT.Copy).then_inc(o_hi_ready, 1)
                for i in range(8):
                    n = N + T_WA + i
                    split_hi(n + 1)
                    if i == 0:
                        act.wait_ge(tile_done, n)
                    act.wait_ge(lru_step, 12 * (8 * l + i + 1))
                    act.activation(l_hi[:, i, :], L[:, i, :], ACT.Copy).then_inc(l_hi_ready, 1)
                for i in range(8):
                    n = N + T_WL + i
                    split_hi(n + 1)
                    act.wait_ge(b_scaled, 8 * l + i + 1)
                    act.activation(m_hi[:, i, :], GB[:, i, :], ACT.Copy).then_inc(m_hi_ready, 1)
                for i in range(8):
                    n = N + T_WO + i
                    split_hi(n + 1)
                    act.wait_ge(evacuated, n + 1)
                    y_square(l, 0, i)
                split_hi(N + T_MLP + 1)
                inverse_rms(rn[:], y_ssq, 2 * l + 1, y_rs, 4 * l, -0.5)
                for k in range(KT):
                    input_tile(l, 1, k)
                for k in range(KT):
                    x_square(l, 1, k)
                for c in range(2):
                    for i in range(16):
                        n = N + T_MLP + 32 * c + i
                        if c + i > 0:
                            split_hi(n + 1)
                        act.wait_ge(evacuated, n + 1)
                        act.activation(T[:, i % 2, :], T[:, i % 2, :], ACT.Square).then_inc(relu2_done, 1)
                        act.wait_ge(relu2_done, 16 * (2 * l + c) + i + 1)
                        act.activation(u_hi[:, i, :], T[:, i % 2, :], ACT.Copy).then_inc(u_hi_ready, 1)
                        if c == 0 and i == 1:
                            inverse_rms(r2q[:], x_ssq, 2 * l + 2, x_rs, 4 * l + 2, -1.0)
                    for m in range(8):
                        n = N + T_MLP + 32 * c + 16 + 2 * m
                        for half in range(2):
                            if n + half + 1 < TL * DEPTH:
                                split_hi(n + half + 1)
                        if c == 1:
                            act.wait_ge(f_scaled, 8 * l + m + 1)
                            y_square(l, 1, m)
                inverse_rms(rn[:], y_ssq, 2 * l + 2, y_rs, 4 * l + 2, -0.5)
                if l + 1 < DEPTH:
                    split_hi(N + TL + 1)
                    for k in range(KT):
                        input_tile(l + 1, 0, k)
                    for k in range(KT):
                        x_square(l + 1, 0, k)
            act.wait_ge(last_turned, 1)
            act.activation(last_t[:], PX[:, 0, 0:P], ACT.Copy).then_inc(last_placed, 1)

        @block.vector
        def _(dve):
            def split_lo(n):
                dve.wait_ge(w_hi_ready, n + 1)
                dve.tensor_tensor(w_lo[:, n % WR, :, :], w_raw[:, n % WR, :, :], w_hi[:, n % 2, :, :].bitcast(F32), ALU.subtract).then_inc(w_lo_ready, 1)

            def input_tile(l, s, k):
                S = 2 * l + s
                dve.wait_ge(h_hi_ready, 8 * S + k + 1)
                dve.scalar_tensor_tensor(out=h_lo[:, k, :], in0=X[:, k, :], scalar=gain(l, k, R_MPRE if s else R_GPRE),
                                         in1=h_hi[:, k, :].bitcast(F32), op0=ALU.mult, op1=ALU.subtract).then_inc(h_lo_ready, 1)

            def x_sum(l, s, k):
                S = 2 * l + s
                if k > 0:
                    dve.wait_ge(x_squared, 8 * S + k + 1)
                    if k > 1:
                        dve.wait_ge(x_summed, 7 * S + k - 1)
                    dve.tensor_tensor(acc_x[:], acc_x[:], sq[:, k % 2, :], ALU.add).then_inc(x_summed, 1)

            def y_sum(l, s, k):
                Y_ = 2 * l + s
                dve.wait_ge(y_squared, 8 * Y_ + k + 1)
                if k > 1:
                    dve.wait_ge(y_summed, 7 * Y_ + k - 1)
                dve.tensor_tensor(acc_y[:], acc_y[:], sq[:, k % 2, :], ALU.add).then_inc(y_summed, 1)

            def update_x(l, s):
                Y_ = 2 * l + s
                dve.wait_ge(y_rs, 4 * l + 2 * s + 2)
                for k in range(KT):
                    dve.scalar_tensor_tensor(out=Y[:, k, :], in0=Y[:, k, :], scalar=gain(l, k, R_MPOST if s else R_GPOST),
                                             in1=rn[:], op0=ALU.mult, op1=ALU.mult).then_inc(y_scaled, 1)
                    if k > 0 and not (s == 1 and l == DEPTH - 1):
                        input_tile(l + s, 1 - s, k - 1)
                    dve.wait_ge(y_scaled, 8 * Y_ + k + 1)
                    dve.tensor_tensor(X[:, k, :], X[:, k, :], Y[:, k, :], ALU.add).then_inc(x_new, 1)
                if not (s == 1 and l == DEPTH - 1):
                    input_tile(l + s, 1 - s, KT - 1)
                    for k in range(1, KT):
                        x_sum(l + s, 1 - s, k)

            def times_rs(dst, n):
                dve.wait_ge(tile_done, n + 1)
                dve.tensor_tensor(halves(dst), proj(n), halves(rs[:]), ALU.mult).then_inc(evacuated, 1)

            def qk_tile(l, p, i):
                g = 4 * l + p
                if i < 2:
                    if p > 0:
                        need(dve, ga_done, 2 * g - 1 + i)
                    else:
                        need(dve, u_lo_ready, 32 * l)
                else:
                    dve.wait_ge(qk_lo_ready, 4 * g + i - 1)
                times_rs(T[:, i % 2, :], TL * l + 12 * p + i)

            def v_rows(l, p, u):
                g = 4 * l + p
                n = TL * l + 12 * p + 4 + u
                dve.wait_ge(tile_done, n + 1)
                dve.wait_ge(stored[u], 32 * (2 * g + 1))
                for grp in range(5):
                    src = PJ[:, n % 2, 1, 0:P] if grp == 0 else PJ[:, n % 2, 0, P * (grp - 1):P * grp]
                    i = dve.tensor_scalar(stage[:, u, grp, :], src, rs_tok[:, grp:grp + 1], None, ALU.mult)
                i.then_inc(evacuated, 1)

            def u_tile(l, p, u):
                g2 = 2 * (4 * l + p) + u
                n = TL * l + 12 * p + 6 + u
                f = 2 * p + u
                dve.tensor_copy(U[:, u, 0:3], par[:, f, 16 * l + R_SC:16 * l + R_SC + 3])
                dve.memset(U[:, u, PR:PR + 3], 0.0)
                dve.memset(U[:, u, 550:552], 0.0)
                dve.wait_ge(tile_done, n + 1)
                dve.tensor_tensor(U[:, u, 3:3 + NS], PJ[:, n % 2, 0, 0:NS], rs[:, 0:NS], ALU.mult)
                dve.tensor_tensor(U[:, u, 38:38 + HT - NS], PJ[:, n % 2, 0, NS:HT], rs[:, NS:HT], ALU.mult)
                dve.tensor_tensor(U[:, u, 38 + HT - NS:38 + NP_], PJ[:, n % 2, 1, 0:HT], rs[:, HT:NT], ALU.mult).then_inc(evacuated, 1)

            def gated_tile(l, p, i):
                g = 4 * l + p
                if i < 2:
                    dve.wait_ge(k_turned, 2 * g + i + 1)
                    dve.wait_ge(qk_lo_ready, 4 * g + 3 + i)
                else:
                    dve.wait_ge(gelu_done, 2 * g + i - 1)
                times_rs(T[:, i % 2, :], TL * l + 12 * p + 8 + i)

            def head_bias(l, p, u):
                h = 2 * p + u
                slope = 2.0 ** (-8.0 * (h + 1) / NHEAD)
                g2 = 2 * (4 * l + p) + u
                need(dve, biased, 10 * g2)
                dve.tensor_scalar(bias_s[:], dist_s[:], -slope / SCALE, None, ALU.mult).then_inc(bias_ready, 1)
                dve.tensor_scalar(bias_p[:], dist_p[:], -slope / SCALE, None, ALU.mult).then_inc(bias_ready, 1)

            def bias_max(l, p, s):
                g = 4 * l + p
                sg, u, qs = 10 * g + s, s // 5, s % 5
                nr, w, b = (NS, NKS, s % 2) if qs == 0 else (P, P * qs, s % 2)
                if qs == 0:
                    dve.wait_ge(bias_ready, 2 * (2 * g + u) + 2)
                if s == 0:
                    dve.wait_ge(stored[0], 32 * (2 * g + 2))
                    dve.wait_ge(stored[1], 32 * (2 * g + 2))
                    dve.wait_ge(v_lo_ready, 2 * g + 2)
                if s >= 3:
                    dve.wait_ge(p_turned, sg - 2)
                need(dve, p_ready, sg - 1)
                dve.wait_ge(scores_done, sg + 1)
                bias = bias_s[:] if qs == 0 else bias_p[:, NP_ - w:NP_]
                for m in range(2):
                    dve.tensor_tensor_reduce(out=s1[0:nr, s % 3, 0:w] if m == 0 else s2[0:nr, b, 0:w], in0=PX[0:nr, m, 0:w], in1=bias,
                                             scale=1.0, scalar=-3.0e38, op0=ALU.add, op1=ALU.max,
                                             accum_out=mx[0:nr, b, m:m + 1]).then_inc(biased, 1)
                dve.wait_ge(biased, 2 * sg + 2)
                dve.tensor_scalar(neg_mx[0:nr, b, :], mx[0:nr, b, :], -SCALE, None, ALU.mult).then_inc(max_ready, 1)

            def combine(l, p, s):
                sg, qs = 10 * (4 * l + p) + s, s % 5
                nr, w, b = (NS, NKS, s % 2) if qs == 0 else (P, P * qs, s % 2)
                p1 = s1[0:nr, s % 3, 0:w]
                dve.wait_ge(exp_done, 2 * sg + 2)
                dve.reciprocal(rl[0:nr, b, :], lsum[0:nr, b, :]).then_inc(norm_step, 1)
                dve.wait_ge(norm_step, 3 * sg + 1)
                dve.tensor_tensor(rl2[0:nr, b:b + 1], rl[0:nr, b, 1:2], neg_lam[0:nr, l:l + 1], ALU.mult).then_inc(norm_step, 1)
                dve.tensor_scalar(p1, p1, rl[0:nr, b, 0:1], None, ALU.mult).then_inc(norm_step, 1)
                dve.wait_ge(norm_step, 3 * sg + 3)
                dve.scalar_tensor_tensor(out=p1, in0=s2[0:nr, b, 0:w], scalar=rl2[0:nr, b:b + 1], in1=p1,
                                         op0=ALU.mult, op1=ALU.add).then_inc(p_ready, 1)

            def p_split(l, p, s):
                sg, qs = 10 * (4 * l + p) + s, s % 5
                nk, w = (3, NS) if qs == 0 else (qs, P)
                dve.wait_ge(pt_hi_ready, sg + 1)
                dve.tensor_tensor(pt_lo[:, 0:nk, 0:w], PX[:, 2, 0:P * nk].rearrange("p (k c) -> p k c", c=P)[:, :, 0:w],
                                  pt_hi[:, 0:nk, 0:w].bitcast(F32), ALU.subtract).then_inc(pt_lo_ready, 1)

            def past_lo(l, p):
                dve.wait_ge(pk_hi_ready, 4 * l + p + 1)
                dve.tensor_tensor(pk_lo[:], PX[:, 2, :].rearrange("p (m c) -> p m c", m=2), pk_hi[:].bitcast(F32), ALU.subtract).then_inc(pk_lo_ready, 1)

            def conv(l, p, u):
                g2, f = 2 * (4 * l + p) + u, 2 * p + u
                dve.wait_ge(conv_first, g2 + 1)
                for j in range(1, CW):
                    if j > 1:
                        dve.wait_ge(conv_step, 3 * g2 + j - 1)
                    dve.scalar_tensor_tensor(out=uc[:], in0=U[:, u, j:j + LW], scalar=gain(l, f, R_CW + j), in1=uc[:],
                                             op0=ALU.mult, op1=ALU.add).then_inc(conv_step, 1)

            def lru_a(l, p, u):
                g2 = 2 * (4 * l + p) + u
                need(dve, lru_step, 12 * g2)
                dve.wait_ge(lru_act, 5 * g2 + 3)
                dve.tensor_tensor(tm[:], aa[:], aa[:], ALU.mult).then_inc(lru_step, 1)
                dve.wait_ge(lru_act, 5 * g2 + 4)
                dve.wait_ge(lru_step, 12 * g2 + 1)
                dve.scalar_tensor_tensor(out=tm[:], in0=tm[:], scalar=1.0, in1=tr[:], op0=ALU.add, op1=ALU.mult).then_inc(lru_step, 1)
                dve.scalar_tensor_tensor(out=ti[:], in0=ti[:], scalar=1.0, in1=uc[:], op0=ALU.add, op1=ALU.mult).then_inc(lru_step, 1)

            def lru_b(l, p, u):
                g2, f = 2 * (4 * l + p) + u, 2 * p + u
                dve.wait_ge(lru_act, 5 * g2 + 5)
                dve.wait_ge(lru_step, 12 * g2 + 3)
                dve.scalar_tensor_tensor(out=ti[:], in0=ti[:], scalar=0.5, in1=tm[:], op0=ALU.mult, op1=ALU.mult).then_inc(lru_step, 1)
                dve.wait_ge(lru_step, 12 * g2 + 4)
                dve.tensor_tensor_scan(tm[:, 0:NS], aa[:, 0:NS], ti[:, 0:NS], gain(l, f, R_SL), ALU.mult, ALU.add).then_inc(lru_step, 1)
                dve.tensor_tensor_scan(tm[:, PR:PR + NP_], aa[:, PR:PR + NP_], ti[:, PR:PR + NP_], 0.0, ALU.mult, ALU.add).then_inc(lru_step, 1)
                dve.tensor_copy(last[:, l, 0:3, f], U[:, u, 547:550]).then_inc(lru_step, 1)
                dve.tensor_copy(last[:, l, 3:6, f], U[:, u, NS:NS + 3]).then_inc(lru_step, 1)
                dve.wait_ge(lru_step, 12 * g2 + 6)
                dve.tensor_copy(last[:, l, 6:7, f], tm[:, PR + NP_ - 1:PR + NP_]).then_inc(lru_step, 1)
                dve.tensor_copy(last[:, l, 7:8, f], tm[:, NS - 1:NS]).then_inc(lru_step, 1)
                dve.wait_ge(gelu_done, g2 + 1)
                dve.tensor_tensor(L[:, f, 0:NS], L[:, f, 0:NS], tm[:, 0:NS], ALU.mult).then_inc(lru_step, 1)
                dve.tensor_tensor(L[:, f, NS:NT], L[:, f, NS:NT], tm[:, PR:PR + NP_], ALU.mult).then_inc(lru_step, 1)

            def sub_norm(l, p, u):
                g2 = 2 * (4 * l + p) + u
                f = 2 * p + u
                dve.wait_ge(o_rs, 2 * g2 + 2)
                dve.scalar_tensor_tensor(out=O[:, f, :], in0=O[:, f, :], scalar=gs[:, l:l + 1], in1=rr[:], op0=ALU.mult, op1=ALU.mult).then_inc(o_normed, 1)

            dve.memset(ones[:], 1.0)
            dve.memset(eps_col[:], EPS)
            dve.memset(s1[:], 0.0)
            dve.wait_ge(const_step, 3)
            lam_init = [0.8 - 0.6 * math.exp(-0.3 * l) for l in range(DEPTH)]
            dve.tensor_scalar(bias_p[:], dist_p[:], -1.0, None, ALU.mult).then_inc(lam_step, 1)
            dve.tensor_scalar(bias_s[:], dist_s[:], -1.0, None, ALU.mult).then_inc(lam_step, 1)
            dve.wait_ge(lam_step, 2)
            dve.tensor_tensor(dist_p[:], dist_p[:], bias_p[:], ALU.max).then_inc(lam_step, 1)
            dve.wait_ge(lam_step, 3)
            dve.tensor_tensor(dist_s[:], dist_s[:], bias_s[:], ALU.max)
            dve.memset(dist_p[0:CHUNK, NP_ - CHUNK:NP_], NEG_DIST)
            dve.wait_ge(lam_landed, 16 * 5 * DEPTH)
            for l in range(DEPTH):
                for j in range(2):
                    i = dve.tensor_tensor_reduce(out=lprod[:], in0=lq[:, l, 2 * j, :], in1=lq[:, l, 2 * j + 1, :], scale=1.0, scalar=0.0,
                                                 op0=ALU.mult, op1=ALU.add, accum_out=lsc[:, 6, 2 * l + j:2 * l + j + 1])
                    if l == DEPTH - 1 and j == 1:
                        i.then_inc(lam_step, 1)
                    else:
                        i.then_inc(norm_chain0, 1)
                        dve.wait_ge(norm_chain0, 2 * l + j + 1)
            for l in range(DEPTH):
                dve.tensor_scalar(gs[:, l:l + 1], gs[:, l:l + 1], 1.0 - lam_init[l], None, ALU.mult)
            dve.wait_ge(par_turned, 1)
            dve.tensor_copy(par[:], PX[:, 0, 0:256].rearrange("p (k r) -> p k r", r=32)).then_inc(par_step, 1)
            dve.wait_ge(par_step, 1)
            for l in range(DEPTH):
                dve.tensor_scalar(half_b[:, l, :, :], par[:, :, 16 * l + R_BR:16 * l + R_BR + 2], 0.5, None, ALU.mult)
            zl = [par[:, :, 16 * l + R_LAM] for l in range(DEPTH)]
            step = [0]

            def link(ins):
                step[0] += 1
                ins.then_inc(sp_step, 1)
                dve.wait_ge(sp_step, step[0])

            for l in range(DEPTH):
                link(dve.tensor_scalar(lsc[:, 2, KT * l:KT * l + KT], zl[l], -1.0, None, ALU.mult))
                link(dve.tensor_tensor(lsc[:, 0, KT * l:KT * l + KT], lsc[:, 2, KT * l:KT * l + KT], zl[l], ALU.max))
            dve.tensor_scalar(lsc[:, 2, :], lsc[:, 2, :], 0.0, None, ALU.max).then_inc(par_step, 1)
            dve.wait_ge(lam_act, 1)
            link(dve.tensor_scalar(lsc[:, 3, :], lsc[:, 1, :], 2.0, None, ALU.add))
            link(dve.reciprocal(lsc[:, 3, :], lsc[:, 3, :]))
            link(dve.tensor_tensor(lsc[:, 3, :], lsc[:, 3, :], lsc[:, 1, :], ALU.mult))
            link(dve.tensor_tensor(lsc[:, 4, :], lsc[:, 3, :], lsc[:, 3, :], ALU.mult))
            terms = 9
            link(dve.tensor_scalar(lsc[:, 5, :], lsc[:, 4, :], 1.0 / (2 * terms - 1), 1.0 / (2 * terms - 3), ALU.mult, ALU.add))
            for t in range(terms - 3, -1, -1):
                link(dve.tensor_tensor(lsc[:, 5, :], lsc[:, 5, :], lsc[:, 4, :], ALU.mult))
                link(dve.tensor_scalar(lsc[:, 5, :], lsc[:, 5, :], 1.0 / (2 * t + 1), None, ALU.add))
            link(dve.tensor_tensor(lsc[:, 5, :], lsc[:, 5, :], lsc[:, 3, :], ALU.mult))
            link(dve.scalar_tensor_tensor(out=lsc[:, 5, :], in0=lsc[:, 5, :], scalar=2.0, in1=lsc[:, 2, :], op0=ALU.mult, op1=ALU.add))
            link(dve.tensor_scalar(cs[:].rearrange("p l k -> p (l k)"), lsc[:, 5, :], -4.0, None, ALU.mult))
            dve.wait_ge(lam_act, 2)
            for l in range(DEPTH):
                link(dve.tensor_tensor(neg_lam[:, l:l + 1], lsc[:, 7, 2 * l + 1:2 * l + 2], lsc[:, 7, 2 * l:2 * l + 1], ALU.subtract))
                link(dve.tensor_scalar(neg_lam[:, l:l + 1], neg_lam[:, l:l + 1], -lam_init[l], None, ALU.add))
            for k in range(KT):
                dve.wait_ge(x_turned, k + 1)
                c = NS + 2 * P
                dve.tensor_copy(X[:, k, 0:c], PJ[:, k % 2, 0, 0:c])
                dve.tensor_copy(X[:, k, c:NT], PJ[:, k % 2, 1, 0:2 * P]).then_inc(x_placed, 1)
            split_lo(0)
            split_lo(1)
            for k in range(KT):
                input_tile(0, 0, k)
            for k in range(1, KT):
                x_sum(0, 0, k)

            for l in range(DEPTH):
                N = TL * l
                for p in range(4):
                    n = N + 12 * p
                    for i in range(6):
                        if not (p == 0 and i == 0):
                            split_lo(n + i + 1)
                        if p == 0 and i == 0:
                            dve.wait_ge(x_rs, 4 * l + 2)
                        if i == 2 and p > 0:
                            lru_a(l, p - 1, 0)
                        if i == 3 and p > 0:
                            conv(l, p - 1, 1)
                            lru_b(l, p - 1, 0)
                        if i < 4:
                            qk_tile(l, p, i)
                        if p == 0 and i == 0:
                            dve.wait_ge(rs_turned, l + 1)
                            dve.tensor_copy(rs_tok[:], PX[:, 3, 0:10].rearrange("p (g c) -> p g c", c=2)[:, :, 0]).then_inc(rs_tok_ready, 1)
                        if i == 0 and p > 0:
                            past_lo(l, p)
                        if i == 3 and p > 0:
                            sub_norm(l, p - 1, 0)
                        if i == 4:
                            if p == 0:
                                dve.wait_ge(rs_tok_ready, l + 1)
                            else:
                                lru_a(l, p - 1, 1)
                            v_rows(l, p, 0)
                        if i == 5:
                            if p == 0:
                                past_lo(l, p)
                            else:
                                lru_b(l, p - 1, 1)
                                sub_norm(l, p - 1, 1)
                            v_rows(l, p, 1)
                    for j in range(12):
                        if j % 2 == 0:
                            split_lo(n + 7 + j // 2)
                        if j in (0, 5):
                            head_bias(l, p, j // 5)
                        if j < 10:
                            bias_max(l, p, j)
                        if 1 <= j < 11:
                            combine(l, p, j - 1)
                        if 2 <= j:
                            p_split(l, p, j - 2)
                        if j in (1, 3):
                            u_tile(l, p, j // 2)
                        if j in (5, 7, 9, 11):
                            gated_tile(l, p, (j - 5) // 2)
                        if j == 10:
                            conv(l, p, 0)
                for i in range(8):
                    n = N + T_GB + i
                    split_lo(n + 1)
                    if i < 2:
                        dve.wait_ge(ga_done, 2 * (4 * l + 3) + i + 1)
                    else:
                        dve.wait_ge(gb_done, 8 * l + i - 1)
                    times_rs(T[:, i % 2, :], n)
                    if i == 1:
                        lru_a(l, 3, 0)
                        conv(l, 3, 1)
                    if i == 2:
                        lru_b(l, 3, 0)
                        sub_norm(l, 3, 0)
                    if i == 3:
                        lru_a(l, 3, 1)
                    if i == 4:
                        lru_b(l, 3, 1)
                        sub_norm(l, 3, 1)
                    for f in o_turns[i]:
                        dve.wait_ge(o_hi_ready, 8 * l + f + 1)
                        dve.tensor_tensor(o_lo[:, f, :], O[:, f, :], o_hi[:, f, :].bitcast(F32), ALU.subtract).then_inc(o_lo_ready, 1)
                for i in range(8):
                    n = N + T_WA + i
                    split_lo(n + 1)
                    dve.wait_ge(l_hi_ready, 8 * l + i + 1)
                    dve.tensor_tensor(l_lo[:, i, :], L[:, i, :], l_hi[:, i, :].bitcast(F32), ALU.subtract).then_inc(l_lo_ready, 1)
                    dve.wait_ge(tile_done, n + 1)
                    dve.wait_ge(ga_done, 8 * (l + 1))
                    dve.scalar_tensor_tensor(out=halves(GA[:, i, :]), in0=halves(GA[:, i, :]), scalar=1.0, in1=proj(n),
                                             op0=ALU.add, op1=ALU.mult).then_inc(evacuated, 1)
                for i in range(8):
                    n = N + T_WL + i
                    split_lo(n + 1)
                    dve.wait_ge(tile_done, n + 1)
                    dve.wait_ge(gb_done, 8 * (l + 1))
                    dve.scalar_tensor_tensor(out=halves(GB[:, i, :]), in0=halves(GB[:, i, :]), scalar=1.0, in1=proj(n),
                                             op0=ALU.add, op1=ALU.mult).then_inc(evacuated, 1)
                    dve.wait_ge(evacuated, n + 1)
                    dve.tensor_tensor(GB[:, i, :], GB[:, i, :], GA[:, i, :], ALU.add).then_inc(b_scaled, 1)
                for i in range(8):
                    n = N + T_WO + i
                    split_lo(n + 1)
                    dve.wait_ge(tile_done, n + 1)
                    dve.tensor_scalar(halves(Y[:, i, :]), proj(n), 0.5, None, ALU.mult).then_inc(evacuated, 1)
                    if i > 1:
                        y_sum(l, 0, i - 1)
                y_sum(l, 0, 7)
                split_lo(N + T_MLP + 1)
                update_x(l, 0)
                for c in range(2):
                    for i in range(16):
                        n = N + T_MLP + 32 * c + i
                        if c + i > 0:
                            split_lo(n + 1)
                        if c == 0 and i < 2:
                            dve.wait_ge(gb_done, 8 * (l + 1))
                        else:
                            dve.wait_ge(u_lo_ready, 16 * (2 * l + c) + i - 1)
                        dve.wait_ge(tile_done, n + 1)
                        dve.tensor_scalar(halves(T[:, i % 2, :]), proj(n), 0.0, None, ALU.max).then_inc(evacuated, 1)
                    for m in range(8):
                        n = N + T_MLP + 32 * c + 16 + 2 * m
                        for half in range(2):
                            if n + half + 1 < TL * DEPTH:
                                split_lo(n + half + 1)
                        dve.wait_ge(tile_done, n + 2)
                        for half in range(2):
                            cl = slice(HT * half, HT * half + HT)
                            if c == 0:
                                dve.tensor_copy(Y[:, m, cl], PJ[:, m % 2, half, 0:HT]).then_inc(evacuated, 1)
                            else:
                                dve.tensor_tensor(Y[:, m, cl], Y[:, m, cl], PJ[:, m % 2, half, 0:HT], ALU.add).then_inc(evacuated, 1)
                        if c == 1:
                            dve.wait_ge(evacuated, n + 2)
                            if m == 0:
                                dve.wait_ge(x_rs, 4 * l + 4)
                            dve.tensor_tensor(Y[:, m, :], Y[:, m, :], r2q[:], ALU.mult).then_inc(f_scaled, 1)
                            if m > 1:
                                y_sum(l, 1, m - 1)
                y_sum(l, 1, 7)
                if l + 1 < DEPTH:
                    split_lo(N + TL + 1)
                update_x(l, 1)
            for grp in range(5):
                dve.wait_ge(out_turned, grp + 1)
                if grp >= 2:
                    dve.wait_ge(out_stored[grp % 2], 16 * (grp // 2))
                nr = NS if grp == 0 else P
                dve.tensor_copy(y_out[0:nr, grp % 2, :].rearrange("p (a b) -> p a b", a=2), PJ[0:nr, grp % 2, :, :]).then_inc(out_placed, 1)


_INS = ["x_prompt", "x_sample", "cache_k", "cache_v", "state_conv", "state_lru", "w_in", "lambda_q1", "lambda_k1", "lambda_q2",
        "lambda_k2", "g_sub", "conv_w", "conv_b", "w_rg", "b_rg", "w_ig", "b_ig", "lru_lambda", "w_branch_attn", "w_branch_lru",
        "w_out", "w_up", "w_down", "g_mix_pre", "g_mix_post", "g_mlp_pre", "g_mlp_post"]


def kernel(**inputs):
    import numpy as _np
    import concourse.bacc as _bacc
    from concourse import mybir as _mybir
    from concourse.bass_utils import run_bass_kernel_spmd as _run

    nc = _bacc.Bacc("TRN2", target_bir_lowering=False, num_devices=1)
    arrays, args = {}, {}
    for name in _INS:
        a = _np.ascontiguousarray(inputs[name])
        arrays[f"in_{name}"] = a
        args[name] = nc.dram_tensor(f"in_{name}", a.shape, _mybir.dt.from_np(a.dtype), kind="ExternalInput").ap()
    L = inputs["w_in"].shape[0]
    outs = [("y_prompt", (1, 512, 1024)), ("y_sample", (1, 32, 1024)), ("prompt_k", (L, 1, 512, 16, 64)),
            ("prompt_v", (L, 1, 512, 8, 128)), ("prompt_conv", (L, 1, 3, 1024)), ("prompt_lru", (L, 1, 1024)),
            ("sample_k", (L, 1, 32, 16, 64)), ("sample_v", (L, 1, 32, 8, 128)), ("sample_conv", (L, 1, 3, 1024)),
            ("sample_lru", (L, 1, 1024))]
    out = {name: nc.dram_tensor(f"out_{name}", shape, _mybir.dt.float32, kind="ExternalOutput").ap() for name, shape in outs}
    hybrid_encoder(nc, args, out)
    r = _run(nc, [arrays], core_ids=[0])
    return tuple(r.results[0][f"out_{name}"] for name, _ in outs)
```

```python
import math
from contextlib import ExitStack

import concourse.bass as bass
from concourse import mybir

P = 128
ALU = mybir.AluOpType
ACT = mybir.ActivationFunctionType
F32 = mybir.dt.float32
F32R = mybir.dt.float32r

EPS = 1e-6
NHEAD = 8
HD = 64
VD = 128
CHUNK = 64
SCALE = HD ** -0.5
KT = 8
NS = 32
NP_ = 512
NT = NS + NP_
HT = NT // 2
PAST = 256
NKS = PAST + NS
CW = 4
LW = 548
LH = LW // 2
PR = 35
WR = 4
TL = 144
T_GB, T_WA, T_WL, T_WO, T_MLP = 48, 56, 64, 72, 80
(R_GPRE, R_GPOST, R_MPRE, R_MPOST, R_CW, R_CB, R_BR, R_BI, R_LAM, R_SC, R_SL) = (0, 1, 2, 3, 4, 8, 9, 10, 11, 12, 15)
NEG_DIST = 2.6e32


def need(eng, sem, value, first=False):
    if first or isinstance(value, int) and value <= 0:
        return
    eng.wait_ge(sem, value)


class TileNo:

    def __init__(self, value, slot):
        self.value, self.slot = value, slot

    def __add__(self, k):
        return TileNo(self.value + k, (self.slot + k) % WR)


def hybrid_encoder(nc, A, out):
    DEPTH = A["w_in"].shape[0]
    with ExitStack() as ctx:
        base = (nc.sbuf_base + 31) // 32 * 32
        arena = {}

        def at(name, shape, dt, offset):
            size = 4
            for s in shape[1:]:
                size *= s
            assert offset + size <= nc.sbuf_usable_end, (name, offset + size)
            arena[name] = (offset, size)
            return nc.alloc_sbuf_tensor_at(name, shape, dt, offset=offset)

        top = [base]

        def room(nbytes):
            o = top[0]
            top[0] += (nbytes + 31) // 32 * 32
            assert top[0] <= nc.sbuf_usable_end, top[0] - nc.sbuf_usable_end
            return o

        def sb(name, shape, dt=F32):
            size = 4
            for s in shape[1:]:
                size *= s
            return at(name, shape, dt, room(size))

        def sem(name):
            return ctx.enter_context(nc.semaphore(name))

        TILE = NT * 4
        X = sb("X", [P, KT, NT])
        W_RAW_AT = room(WR * KT * P * 4)
        w_raw = at("w_raw", [P, WR, KT, P], F32, W_RAW_AT)
        w_lo = at("w_lo", [P, WR, KT, P], F32R, W_RAW_AT)
        w_hi = sb("w_hi", [P, 2, KT, P], F32R)
        ident = sb("ident", [P, P])
        ones = sb("ones", [P, P])
        dist_p = sb("dist_p", [P, NP_])
        dist_s = sb("dist_s", [NS, NKS])
        bias_p = sb("bias_p", [P, NP_])
        bias_s = sb("bias_s", [NS, NKS])
        par = sb("par", [P, KT, 32])
        gs = sb("gs", [P, 2])
        neg_lam = sb("neg_lam", [P, 2])
        eps_col = sb("eps_col", [P, 1])
        warm = sb("warm", [P, 1])
        rs_tok = sb("rs_tok", [P, 5])
        mx = sb("mx", [P, 2, 2])
        neg_mx = sb("neg_mx", [P, 2, 2])
        lsum = sb("lsum", [P, 2, 2])
        rl = sb("rl", [P, 2, 2])
        rl2 = sb("rl2", [P, 2])
        rs = sb("rs", [P, NT])
        last = sb("last", [P, 2, 8, KT])
        w_gate = sb("w_gate", [P, 2, 2, P])
        T = sb("T", [P, 2, NT])

        H_AT = room(2 * KT * TILE)
        h_hi = at("h_hi", [P, KT, NT], F32R, H_AT)
        h_lo = at("h_lo", [P, KT, NT], F32R, H_AT + KT * TILE)
        l_hi = at("l_hi", [P, KT, NT], F32R, H_AT)
        m_hi = at("m_hi", [P, KT, NT], F32R, H_AT + KT * TILE)
        BIG = room(4 * KT * TILE)
        O = at("O", [P, KT, NT], F32, BIG)
        o_lo = at("o_lo", [P, KT, NT], F32R, BIG)
        L = at("L", [P, KT, NT], F32, BIG + KT * TILE)
        l_lo = at("l_lo", [P, KT, NT], F32R, BIG + KT * TILE)
        GA = at("GA", [P, KT, NT], F32, BIG + 2 * KT * TILE)
        m_lo = at("m_lo", [P, KT, NT], F32R, BIG + 2 * KT * TILE)
        qk_hi = at("qk_hi", [P, 4, NT], F32R, BIG + 3 * KT * TILE)
        qk_lo = at("qk_lo", [P, 4, NT], F32R, BIG + 3 * KT * TILE + 4 * TILE)
        GB = at("GB", [P, KT, NT], F32, BIG + 3 * KT * TILE)
        u_hi = at("u_hi", [P, 16, NT], F32R, BIG)
        u_lo = at("u_lo", [P, 16, NT], F32R, BIG + 16 * TILE)
        V_AT = room(5 * 256 * 4 * 2 + 8192)
        v_hi = at("v_hi", [P, 5, 2, VD], F32R, V_AT)
        v_lo = at("v_lo", [P, 5, 2, VD], F32R, V_AT + 5120)
        pk_hi = at("pk_hi", [P, 2, PAST], F32R, V_AT + 10240)
        pk_lo = at("pk_lo", [P, 2, PAST], F32R, V_AT + 12288)
        pv_hi = at("pv_hi", [P, 2, 2 * VD], F32R, V_AT + 14336)
        pv_lo = at("pv_lo", [P, 2, 2 * VD], F32R, V_AT + 16384)
        o_hi = at("o_hi", [P, KT, NT], F32R, V_AT)
        Y = at("Y", [P, KT, NT], F32, V_AT)
        S_AT = room(14336)
        s1 = at("s1", [P, 3, 512], F32, S_AT)
        s2 = at("s2", [P, 2, 512], F32, S_AT + 6144)
        pt_hi = at("pt_hi", [P, 4, P], F32R, S_AT + 10240)
        pt_lo = at("pt_lo", [P, 4, P], F32R, S_AT + 12288)
        stage = at("stage", [P, 2, 5, P], F32, S_AT)
        sq_o = at("sq_o", [P, NT], F32, S_AT + 5120)
        rr = at("rr", [P, NT], F32, S_AT + 5120 + TILE)
        R_AT = room(7 * 552 * 4)
        U = at("U", [P, 2, 552], F32, R_AT)
        o_ = R_AT + 2 * 552 * 4
        uc, tr, aa, ti, tm = (at(n, [P, LW], F32, o_ + i * 552 * 4) for i, n in enumerate(["uc", "tr", "aa", "ti", "tm"]))
        pk_raw = at("pk_raw", [P, 2, 2, P], F32, o_ + 3 * 552 * 4)
        pv_raw = at("pv_raw", [P, 2, 2 * VD], F32, o_ + 4 * 552 * 4)
        acc_x = at("acc_x", [P, NT], F32, R_AT)
        acc_y = at("acc_y", [P, NT], F32, R_AT + TILE)
        sq = at("sq", [P, 2, NT], F32, R_AT + 2 * TILE)
        rn = at("rn", [P, NT], F32, R_AT + 4 * TILE)
        r2q = at("r2q", [P, NT], F32, R_AT + 5 * TILE)
        x_in = at("x_in", [P, 5, KT * P], F32, BIG)
        rows = at("rows", [32, KT * P], F32, BIG + 5 * 4096)
        lq = at("lq", [P, 2, 4, HD], F32, BIG + 6 * 4096)
        lprod = at("lprod", [P, HD], F32, BIG + 7 * 4096)
        lsc = at("lsc", [P, 8, KT * 2], F32, BIG + 7 * 4096 + 256)
        y_out = at("y_out", [P, 5, 2, 512], F32, BIG)
        last_t = at("last_t", [P, P], F32, BIG + 5 * 4096)

        PJ = ctx.enter_context(nc.psum_tensor("PJ", [P, 2, 2, 512], F32))
        PX = ctx.enter_context(nc.psum_tensor("PX", [P, 4, 512], F32))

        w_landed = [sem(f"w_landed{i}") for i in range(WR)]
        w_hi_ready, w_lo_ready, tile_done, evacuated = map(sem, ("w_hi_ready", "w_lo_ready", "tile_done", "evacuated"))
        x_landed, par_landed, lam_landed = map(sem, ("x_landed", "par_landed", "lam_landed"))
        const_step, ident_ready = sem("const_step"), sem("ident_ready")
        lambda_chain, param_chain = sem("lambda_chain"), sem("param_chain")
        x_turned, par_turned, par_step, lam_step, lam_act = map(
            sem, ("x_turned", "par_turned", "par_step", "lam_step", "lam_act"))
        h_hi_ready, h_lo_ready, x_squared, x_summed, x_ssq, x_rs = map(
            sem, ("h_hi_ready", "h_lo_ready", "x_squared", "x_summed", "x_ssq", "x_rs"))
        y_squared, y_summed, y_ssq, y_rs, y_scaled, x_new = map(
            sem, ("y_squared", "y_summed", "y_ssq", "y_rs", "y_scaled", "x_new"))
        rs_turned, rs_tok_ready = sem("rs_turned"), sem("rs_tok_ready")
        qk_hi_ready, qk_lo_ready, k_turned, k_staged = map(sem, ("qk_hi_ready", "qk_lo_ready", "k_turned", "k_staged"))
        v_hi_ready, v_lo_ready = sem("v_hi_ready"), sem("v_lo_ready")
        stored = [sem("stored0"), sem("stored1")]
        past_landed, past_turned, pk_hi_ready, pk_lo_ready, pv_hi_ready, pv_lo_ready = map(
            sem, ("past_landed", "past_turned", "pk_hi_ready", "pk_lo_ready", "pv_hi_ready", "pv_lo_ready"))
        bias_ready, scores_done, biased, max_ready, exp_done, norm_step, p_ready = map(
            sem, ("bias_ready", "scores_done", "biased", "max_ready", "exp_done", "norm_step", "p_ready"))
        p_turned, pt_hi_ready, pt_lo_ready, pv_done, o_placed = map(
            sem, ("p_turned", "pt_hi_ready", "pt_lo_ready", "pv_done", "o_placed"))
        o_squared, o_ssq, o_rs, o_normed, o_hi_ready, o_lo_ready = map(
            sem, ("o_squared", "o_ssq", "o_rs", "o_normed", "o_hi_ready", "o_lo_ready"))
        wg_zero, wg_landed, conv_first, conv_step, gates_done, lru_act, lru_step = map(
            sem, ("wg_zero", "wg_landed", "conv_first", "conv_step", "gates_done", "lru_act", "lru_step"))
        gelu_done, ga_done, gb_done, l_hi_ready, l_lo_ready, b_scaled, m_hi_ready, m_lo_ready = map(
            sem, ("gelu_done", "ga_done", "gb_done", "l_hi_ready", "l_lo_ready", "b_scaled", "m_hi_ready", "m_lo_ready"))
        relu2_done, u_hi_ready, u_lo_ready, f_scaled = map(sem, ("relu2_done", "u_hi_ready", "u_lo_ready", "f_scaled"))
        out_turned, last_turned, last_placed, out_stored = map(sem, ("out_turned", "last_turned", "last_placed", "out_stored"))
        out_placed = [sem("out_placed0"), sem("out_placed1")]
        last_stored = sem("last_stored")

        def own_wait(eng):
            eng.nop(nofuse=True)

        def out_bank(b):
            b = b % 8
            return PJ[:, b // 2, b % 2, :] if b < 4 else PX[:, b - 4, :]

        def mixer_tile(l, first, r, j):
            return TileNo(TL * l + first + 4 * r + j, j)

        def mlp_tile(l, c, later, j):
            return TileNo(TL * l + (T_MLP + 32 * c) + later + j, j)

        def halves(t):
            return t.rearrange("p (a b) -> p a b", a=2)

        def cols(g):
            return slice(0, P) if g == 0 else slice(NS + P * (g - 1), NS + P * g)

        def proj(n):
            return PJ[:, n.slot % 2, :, 0:HT]

        def gain(k, row):
            return par[:, k, row:row + 1]

        def columns(name, l, block):
            return A[name].rearrange("l (k p) (b n) -> l b p k n", p=P, n=P)[l, block]

        def pair_source(l, p, j):
            return columns("w_in", l, 4 * j + p if j < 4 else 16 + 8 * ((j - 4) // 2) + 2 * p + j % 2)

        o_turns = [(0,), (1, 2), (3,), (), (4,), (5, 6), (), (7,)]

        def down_source(l, c, half, m):
            return A["w_down"].rearrange("l (c h k p) (m n) -> l c h m p k n", c=2, h=2, p=P, n=P)[l, c, half, m]

        block = ctx.enter_context(nc.Block())

        PAR_DMAS = 9 + 2 * DEPTH

        @block.sync
        def _(sp):
            sp.dma_start(x_in[0:NS, 0, :], A["x_sample"][0]).then_inc(x_landed, 16)
            sp.dma_start(x_in[:, 1:5, :], A["x_prompt"][0].rearrange("(g t) d -> t g d", t=P)).then_inc(x_landed, 16)

            def load(n, source):
                sp.wait_ge(tile_done, n.value - WR + 1)
                sp.dma_start(w_raw[:, n.slot, :, :], source).then_inc(w_landed[n.slot], 16)

            def load_layer(l):
                def pair(p, first=0):
                    for j in range(first, 12):
                        load(TileNo(TL * l + 12 * p + j, j % WR), pair_source(l, p, j))

                pair(0, WR)
                with sp.Fori(1, 4) as p:
                    pair(p)
                for first, name, block in ((T_GB, "w_in", 48), (T_WA, "w_branch_attn", 0), (T_WL, "w_branch_lru", 0), (T_WO, "w_out", 0)):
                    with sp.Fori(0, KT // WR) as r:
                        for j in range(WR):
                            load(TileNo(TL * l + first + WR * r + j, j), columns(name, l, block + WR * r + j))
                for c in range(2):
                    with sp.Fori(0, 4) as r:
                        for j in range(WR):
                            load(mlp_tile(l, c, 4 * r, j), columns("w_up", l, 16 * c + 4 * r + j))
                    with sp.Fori(0, 4) as r:
                        for j in range(WR):
                            load(mlp_tile(l, c, 16 + 4 * r, j), down_source(l, c, j % 2, 2 * r + j // 2))

            for i in range(WR):
                sp.dma_start(w_raw[:, i, :, :], pair_source(0, 0, i)).then_inc(w_landed[i], 16)
            with sp.Fori(0, DEPTH - 1) as l:
                load_layer(l)
                for i in range(WR):
                    load(TileNo(TL * l + TL + i, i), pair_source(l + 1, 0, i))
            load_layer(DEPTH - 1)
            for g in range(5):
                sp.wait_ge(out_placed[0], g + 1)
                sp.wait_ge(out_placed[1], g + 1)
                to = out["y_sample"][0] if g == 0 else out["y_prompt"][0, P * (g - 1):P * g, :]
                sp.dma_start(to, y_out[0:NS if g == 0 else P, g, :, :].rearrange("p a b -> p (a b)")).then_inc(out_stored, 16)
            sp.wait_ge(out_stored, 16 * 5)

        @block.gpsimd
        def _(pool):
            pool.memset(ident[:], 0.0).then_inc(const_step, 1)
            pool.wait_ge(const_step, 1)
            pool.affine_select(out=ident[:], in_=ident[:], compare_op=ALU.not_equal, fill=1.0, base=0,
                               pattern=[[-1, P]], channel_multiplier=1).then_inc(ident_ready, 1)
            pool.iota(dist_p[:], [[-1, NP_]], base=NP_ - P, channel_multiplier=1,
                      allow_small_or_imprecise_dtypes=True).then_inc(const_step, 1)
            pool.iota(dist_s[:], [[-1, NKS]], base=PAST, channel_multiplier=1,
                      allow_small_or_imprecise_dtypes=True).then_inc(const_step, 1)
            pool.memset(w_gate[:], 0.0).then_inc(wg_zero, 1)
            for l in range(DEPTH):
                for j, name in enumerate(("lambda_q1", "lambda_k1", "lambda_q2", "lambda_k2")):
                    pool.dma_start(lq[:, l, j, :], A[name][l].partition_broadcast(P)).then_inc(lam_landed, 16)
                with nc.allow_non_contiguous_dma(reason="128 values"):
                    pool.dma_start(gs[:, l:l + 1], A["g_sub"][l].rearrange("(p o) -> p o", o=1)).then_inc(lam_landed, 16)

            def load_gate_weights(l, p):
                g = 4 * l + p
                need(pool, wg_zero, 1)
                need(pool, gates_done, 2 * g, first=p == 0)
                own_wait(pool)
                for u in range(2):
                    for j, name in enumerate(("w_rg", "w_ig")):
                        for b in range(2):
                            pool.dma_start(w_gate[64 * b:64 * b + 64, u, j, 64 * b:64 * b + 64],
                                           A[name][l, 4 * p + 2 * u + b]).then_inc(wg_landed, 16)

            def load_past(l, p):
                g = 4 * l + p
                need(pool, past_turned, g, first=p == 0)
                need(pool, pv_lo_ready, g, first=p == 0)
                if p > 0:
                    need(pool, lru_step, 24 * (g - 1), first=p == 1)
                else:
                    pool.wait_ge(x_new, 8 * (2 * l + 1))
                own_wait(pool)
                for m in range(2):
                    pool.dma_start(pk_raw[:, :, m, :], A["cache_k"][l, 0].rearrange("(a t) (m h) d -> m t a (h d)", t=P, m=2)[m][
                        :, :, P * p:P * p + P]).then_inc(past_landed, 16)
                pool.dma_start(pv_raw[:], A["cache_v"][l, 0].rearrange("(a t) h d -> t a (h d)", t=P)[
                    :, :, 256 * p:256 * p + 256]).then_inc(past_landed, 16)

            def update_x(l, s):
                for k in range(KT):
                    pool.wait_ge(y_scaled, 8 * (2 * l + s) + k + 1)
                    pool.tensor_tensor(X[:, k, :], X[:, k, :], Y[:, k, :], ALU.add).then_inc(x_new, 1)

            def past_lo(g):
                pool.wait_ge(pv_hi_ready, g + 1)
                pool.tensor_tensor(pv_lo[:], pv_raw[:], pv_hi[:].bitcast(F32), ALU.subtract).then_inc(pv_lo_ready, 1)

            def store_rows(l, p, j):
                g = 4 * l + p
                if j < 2:
                    pool.wait_ge(k_staged, 2 * g + j + 1)
                    c = 512 * j + P * p
                    to_p = out["prompt_k"][l, 0].rearrange("(g t) h d -> t g (h d)", t=P)[:, :, c:c + P]
                    to_s = out["sample_k"][l, 0].rearrange("t h d -> t (h d)")[:, c:c + P]
                else:
                    pool.wait_ge(evacuated, TL * l + 12 * p + 2 + j + 1)
                    h = 2 * p + j - 2
                    to_p = out["prompt_v"][l, 0].rearrange("(g t) h d -> t g (h d)", t=P)[:, :, VD * h:VD * h + VD]
                    to_s = out["sample_v"][l, 0].rearrange("t h d -> t (h d)")[:, VD * h:VD * h + VD]
                own_wait(pool)
                pool.dma_start(to_p, stage[:, j % 2, 1:5, :]).then_inc(stored[j % 2], 16)
                pool.dma_start(to_s, stage[0:NS, j % 2, 0, :]).then_inc(stored[j % 2], 16)

            with pool.Fori(0, DEPTH) as l:
                for p in range(4):
                    g = 4 * l + p
                    if p == 0:
                        load_past(l, 0)
                    else:
                        past_lo(g)
                    for i in range(4):
                        pool.wait_ge(qk_hi_ready, 4 * g + i + 1)
                        pool.tensor_tensor(qk_lo[:, i, :], T[:, i % 2, :], qk_hi[:, i, :].bitcast(F32), ALU.subtract).then_inc(qk_lo_ready, 1)
                        if i >= 2:
                            store_rows(l, p, i - 2)
                    if p == 0:
                        past_lo(g)
                    for u in range(2):
                        store_rows(l, p, 2 + u)
                        pool.wait_ge(v_hi_ready, 2 * g + u + 1)
                        pool.tensor_tensor(v_lo[:, :, u, :], stage[:, u, :, :], v_hi[:, :, u, :].bitcast(F32), ALU.subtract).then_inc(v_lo_ready, 1)
                    if p < 3:
                        load_past(l, p + 1)
                    load_gate_weights(l, p)
                with pool.Fori(0, KT) as i:
                    pool.wait_ge(m_hi_ready, KT * l + i + 1)
                    own_wait(pool)
                    pool.tensor_tensor(m_lo[:, i, :], GB[:, i, :], m_hi[:, i, :].bitcast(F32), ALU.subtract).then_inc(m_lo_ready, 1)
                update_x(l, 0)
                for c in range(2):
                    with pool.Fori(0, 4) as r:
                        for j in range(4):
                            i = 4 * r + j
                            pool.wait_ge(u_hi_ready, 32 * l + 16 * c + i + 1)
                            own_wait(pool)
                            pool.tensor_tensor(u_lo[:, i, :], T[:, j % 2, :], u_hi[:, i, :].bitcast(F32), ALU.subtract).then_inc(u_lo_ready, 1)
                update_x(l, 1)
            pool.wait_ge(stored[0], 32 * 2 * 4 * DEPTH)
            pool.wait_ge(stored[1], 32 * 2 * 4 * DEPTH)
            pool.wait_ge(last_placed, 1)
            for l in range(DEPTH):
                for r, name, n in ((0, "prompt_conv", 3), (3, "sample_conv", 3), (6, "prompt_lru", 1), (7, "sample_lru", 1)):
                    q = (l * 8 + r) * KT
                    dst = out[name][l, 0].rearrange("r (k c) -> (r k) c", c=P) if n == 3 else out[name][l, 0].rearrange("(k c) -> k c", c=P)
                    pool.dma_start(dst, last_t[q:q + n * KT, :]).then_inc(last_stored, 16)
            pool.wait_ge(last_stored, 16 * 4 * DEPTH)

        @block.tensor
        def _(pe):
            def split_product(ps, w, x, start, stop, mms):
                for a, b in ((0, 0), (0, 1), (1, 0)):
                    for o, c in mms:
                        mm = pe.matmul(o, w[a], x[b][c], start=start and a + b == 0, stop=stop and a == 1)
                return mm

            def tile_in(n):
                pe.wait_ge(w_lo_ready, n.value + 1)

            def gemm(n, src, k0, buf, free, first=True, end=True, ks=range(KT), waits=None):
                if ks[0] == 0:
                    tile_in(n)
                    need(pe, evacuated, free)
                for k in ks:
                    if waits is not None:
                        pe.wait_ge(waits[0], waits[1] + k)
                    w = (w_hi[:, n.slot % 2, k, :], w_lo[:, n.slot, k, :])
                    for a, b in ((0, 0), (0, 1), (1, 0)):
                        for half in range(2):
                            mm = pe.matmul(PJ[:, buf, half, 0:HT], w[a], src[b][:, k0 + k, HT * half:HT * half + HT],
                                           start=first and k == 0 and a + b == 0, stop=end and k == KT - 1 and a == 1)
                if ks[-1] == KT - 1:
                    mm.then_inc(tile_done, 1)

            H = (h_hi, h_lo)

            def gemm_pair(n, free, waits):
                tile_in(n)
                tile_in(n + 1)
                need(pe, evacuated, free)
                for k in range(KT):
                    pe.wait_ge(waits[0], waits[1] + k)
                    for m in (n, n + 1):
                        w = (w_hi[:, m.slot % 2, k, :], w_lo[:, m.slot, k, :])
                        for a, b in ((0, 0), (0, 1), (1, 0)):
                            for half in range(2):
                                mm = pe.matmul(PJ[:, m.slot % 2, half, 0:HT], w[a], H[b][:, k, HT * half:HT * half + HT],
                                               start=k == 0 and a + b == 0, stop=k == KT - 1 and a == 1)
                        if k == KT - 1:
                            mm.then_inc(tile_done, 1)

            def ones_sum(src, bank=0):
                for half in range(2):
                    mm = pe.matmul(PX[:, bank + half, 0:HT], ones[:], src[:, HT * half:HT * half + HT], start=True, stop=True)
                return mm

            def gates(l, p, u):
                g2 = 2 * (4 * l + p) + u
                pe.wait_ge(wg_landed, 16 * 8 * (4 * l + p + 1))
                pe.wait_ge(conv_step, 3 * g2 + 3)
                need(pe, lru_act, 5 * g2, first=p + u == 0)
                for j in range(2):
                    for half in range(2):
                        mm = pe.matmul(PX[:, 2 * j + half, 0:LH], w_gate[:, u, j, :], uc[:, LH * half:LH * half + LH], start=True, stop=True)
                mm.then_inc(gates_done, 1)

            def sub_ssq(l, p, u):
                g2 = 2 * (4 * l + p) + u
                pe.wait_ge(o_squared, g2 + 1)
                pe.wait_ge(lru_act, 5 * g2 + 2)
                ones_sum(sq_o, 2).then_inc(o_ssq, 1)

            def turn_k(l, p, m):
                g = 4 * l + p
                n = TileNo(TL * l, 0) + 12 * p + 2 + m
                pe.wait_ge(evacuated, n.value + 1)
                need(pe, k_staged, 2 * g + m, first=p + m == 0)
                if p > 0:
                    pe.wait_ge(lru_act, 10 * g - 9 + 5 * m)
                for grp in range(5):
                    o = PX[:, 1, 0:P] if grp == 0 else PX[:, 0, P * (grp - 1):P * grp]
                    mm = pe.transpose(o, T[:, m % 2, cols(grp)], ident[:])
                mm.then_inc(k_turned, 1)

            def turn_past(l, p):
                g = 4 * l + p
                pe.wait_ge(past_landed, 48 * (g + 1))
                need(pe, pt_lo_ready, 10 * g, first=p == 0)
                for m in range(2):
                    for a in range(2):
                        mm = pe.transpose(PX[:, 2, 256 * m + P * a:256 * m + P * a + P], pk_raw[:, a, m, :], ident[:])
                mm.then_inc(past_turned, 1)

            def v_tile(l, p, u):
                n = TileNo(TL * l, 0) + 12 * p + 4 + u
                tile_in(n)
                need(pe, evacuated, n.value - 1)
                for grp in range(5):
                    o = PJ[:, n.slot % 2, 1, 0:P] if grp == 0 else PJ[:, n.slot % 2, 0, P * (grp - 1):P * grp]
                    for k in range(KT):
                        w = (w_hi[:, n.slot % 2, k, :], w_lo[:, n.slot, k, :])
                        for a, b in ((0, 0), (0, 1), (1, 0)):
                            mm = pe.matmul(o, H[a][:, k, cols(grp)], w[b], start=k == 0 and a + b == 0, stop=k == KT - 1 and a == 1)
                mm.then_inc(tile_done, 1)

            def scores(l, p, s):
                g = 4 * l + p
                sg, u, qs = 10 * g + s, s // 5, s % 5
                r = slice(HD * u, HD * u + HD)
                if s == 0:
                    pe.wait_ge(qk_lo_ready, 4 * g + 4)
                    pe.wait_ge(pk_lo_ready, g + 1)
                    pe.wait_ge(k_staged, 2 * g + 2)
                need(pe, biased, 2 * sg, first=p + s == 0)
                QK = (qk_hi, qk_lo)
                PK = (pk_hi, pk_lo)
                for m in range(2):
                    if qs == 0:
                        for a, b in ((0, 0), (0, 1), (1, 0)):
                            pe.matmul(PX[:, m, 0:PAST], QK[a][r, m, 0:P], PK[b][r, m, :], start=a + b == 0, stop=a == 1)
                        for a, b in ((0, 0), (0, 1), (1, 0)):
                            mm = pe.matmul(PX[:, m, PAST:NKS], QK[a][r, m, 0:P], QK[b][r, 2 + m, 0:NS], start=a + b == 0, stop=a == 1)
                    else:
                        kw = P * qs
                        for a, b in ((0, 0), (0, 1), (1, 0)):
                            mm = pe.matmul(PX[:, m, 0:kw], QK[a][r, m, cols(qs)], QK[b][r, 2 + m, NS:NS + kw], start=a + b == 0, stop=a == 1)
                mm.then_inc(scores_done, 1)

            def turn_p(l, p, s):
                sg, u, qs = 10 * (4 * l + p) + s, s // 5, s % 5
                pe.wait_ge(p_ready, sg + 1)
                need(pe, pt_lo_ready, sg, first=p + s == 0)
                if s == 0 and p > 0:
                    pe.wait_ge(o_rs, 4 * g - 1)
                src = s1[:, s % 3, :]
                if qs == 0:
                    own_wait(pe)
                    for kt in range(3):
                        mm = pe.transpose(PX[:, 2, P * kt:P * kt + NS], src[0:NS, P * kt:P * kt + P], ident[0:NS, 0:NS])
                else:
                    for kt in range(qs):
                        mm = pe.transpose(PX[:, 2, P * kt:P * kt + P], src[:, P * kt:P * kt + P], ident[:])
                mm.then_inc(p_turned, 1)

            def weigh_v(l, p, s):
                g = 4 * l + p
                sg, u, qs = 10 * g + s, s // 5, s % 5
                if s == 0:
                    pe.wait_ge(v_lo_ready, 2 * g + 2)
                    pe.wait_ge(pv_lo_ready, g + 1)
                pe.wait_ge(pt_lo_ready, sg + 1)
                need(pe, o_placed, sg, first=p + s == 0)
                V, PV, PT = (v_hi, v_lo), (pv_hi, pv_lo), (pt_hi, pt_lo)
                kts = range(3) if qs == 0 else range(qs)
                w = NS if qs == 0 else P
                for kt in kts:
                    for a, b in ((0, 0), (0, 1), (1, 0)):
                        if qs > 0:
                            v, pt = V[a][:, 1 + kt, u, :], PT[b][:, kt, :]
                        elif kt < 2:
                            v, pt = PV[a][:, kt, VD * u:VD * u + VD], PT[b][:, kt, 0:NS]
                        else:
                            v, pt = V[a][0:NS, 0, u, :], PT[b][0:NS, 2, 0:NS]
                        mm = pe.matmul(PX[:, 3, 0:w], v, pt, start=kt == 0 and a + b == 0, stop=kt == kts[-1] and a == 1)
                mm.then_inc(pv_done, 1)

            def up_four(l, c, r):
                first = isinstance(r, int)
                for j in range(4):
                    n = mlp_tile(l, c, 4 * r, j)
                    if first and c == 0 and j == 0:
                        gemm_pair(n, n.value, (h_lo_ready, 8 * (2 * l + 1) + 1))
                    elif not (first and c == 0 and j == 1):
                        gemm(n, H, 0, j % 2, n.value - 2 if first and j == 0 else n.value - 1)

            def down_four(l, c, r):
                first = isinstance(r, int)
                for j in range(4):
                    n = mlp_tile(l, c, 16 + 4 * r, j)
                    half, fresh = j % 2, first and j < 2
                    gemm(n, (u_hi, u_lo), 8 * half, j // 2, (n.value - 1 if fresh else n.value - 2) if half == 0 else 0,
                         first=half == 0, end=half == 1,
                         waits=(u_lo_ready, 16 * (2 * l + c) + 8 * half + 1) if fresh else None)

            pe.wait_ge(ident_ready, 1)
            pe.wait_ge(par_landed, 16 * PAR_DMAS)
            for k in range(KT):
                mm = pe.transpose(PX[:, 0, 32 * k:32 * k + 32], rows[0:32, P * k:P * k + P], ident[0:32, 0:32])
            mm.then_inc(par_turned, 1)
            pe.wait_ge(x_landed, 32)
            for k in range(KT):
                need(pe, x_new, k - 1)
                for grp in range(5):
                    if grp == 0:
                        o = PJ[:, k % 2, 0, 0:NS]
                    else:
                        o = PJ[:, k % 2, (grp - 1) // 2, (NS if grp < 3 else 0) + P * ((grp - 1) % 2):][:, 0:P]
                    if grp == 0:
                        mm = pe.transpose(o, x_in[0:NS, 0, P * k:P * k + P], ident[0:NS, 0:NS])
                    else:
                        mm = pe.transpose(o, x_in[:, grp, P * k:P * k + P], ident[:])
                mm.then_inc(x_turned, 1)
            pe.wait_ge(x_new, KT)

            with pe.Fori(0, DEPTH) as l:
                N = TileNo(TL * l, 0)
                for p in range(4):
                    g, n = 4 * l + p, N + 12 * p
                    if p == 0:
                        gemm_pair(n, 0, (h_lo_ready, 8 * 2 * l + 1))
                        pe.wait_ge(x_summed, 7 * 2 * l + 7)
                        ones_sum(acc_x).then_inc(x_ssq, 1)
                        pe.wait_ge(x_rs, 4 * l + 2)
                        for grp in range(5):
                            mm = pe.matmul(PX[:, 3, 2 * grp:2 * grp + 2], rs[:, cols(grp)], ident[:, 0:2], start=True, stop=True)
                        mm.then_inc(rs_turned, 1)
                    else:
                        gemm(n, H, 0, 0, n.value - 1)
                        weigh_v(l, p - 1, 9)
                        turn_past(l, p)
                        gemm(n + 1, H, 0, 1, n.value)
                        pe.wait_ge(pk_lo_ready, g + 1)
                        gates(l, p - 1, 0)
                    gemm(n + 2, H, 0, 0, n.value + 1)
                    if p > 0:
                        sub_ssq(l, p - 1, 0)
                    gemm(n + 3, H, 0, 1, n.value + 2, ks=range(0, 4))
                    turn_k(l, p, 0)
                    gemm(n + 3, H, 0, 1, n.value + 2, ks=range(4, 8))
                    if p > 0:
                        pe.wait_ge(o_rs, 4 * g - 3)
                        pe.wait_ge(k_staged, 2 * g + 1)
                        gates(l, p - 1, 1)
                    v_tile(l, p, 0)
                    turn_k(l, p, 1)
                    if p == 0:
                        turn_past(l, p)
                    else:
                        sub_ssq(l, p - 1, 1)
                    v_tile(l, p, 1)
                    for j in range(12):
                        i = n + (6 + j // 2)
                        gemm(i, H, 0, i.slot % 2, i.value - 1, ks=range(4 * (j % 2), 4 * (j % 2) + 4))
                        if j >= 3:
                            weigh_v(l, p, j - 3)
                        if j < 10:
                            scores(l, p, j)
                        if j >= 2:
                            turn_p(l, p, j - 2)
                g = 4 * l + 3
                for i in range(8):
                    n = N + (T_GB + i)
                    gemm(n, H, 0, n.slot % 2, n.value - 1)
                    if i == 0:
                        weigh_v(l, 3, 9)
                        pe.wait_ge(o_placed, 10 * (g + 1))
                    if i == 1:
                        gates(l, 3, 0)
                    if i == 2:
                        sub_ssq(l, 3, 0)
                    if i == 4:
                        pe.wait_ge(o_rs, 2 * (2 * g) + 1)
                        gates(l, 3, 1)
                    if i == 5:
                        sub_ssq(l, 3, 1)
                for first, src, ready in ((T_WA, (o_hi, o_lo), o_lo_ready), (T_WL, (l_hi, l_lo), l_lo_ready), (T_WO, (m_hi, m_lo), m_lo_ready)):
                    with pe.Fori(0, KT // 4) as r:
                        for j in range(4):
                            n = mixer_tile(l, first, r, j)
                            gemm(n, src, 0, j % 2, n.value - 1, waits=(ready, 8 * l + 1) if j == 0 else None)
                pe.wait_ge(y_summed, 7 * 2 * l + 7)
                ones_sum(acc_y).then_inc(y_ssq, 1)
                for c in range(2):
                    up_four(l, c, 0)
                    with pe.Fori(1, 4) as r:
                        up_four(l, c, r)
                    if c == 0:
                        pe.wait_ge(x_summed, 7 * (2 * l + 1) + 7)
                        pe.wait_ge(y_rs, 4 * l + 2)
                        ones_sum(acc_x).then_inc(x_ssq, 1)
                    down_four(l, c, 0)
                    with pe.Fori(1, 4) as r:
                        down_four(l, c, r)
                pe.wait_ge(y_summed, 7 * (2 * l + 1) + 7)
                pe.wait_ge(x_rs, 4 * l + 4)
                ones_sum(acc_y).then_inc(y_ssq, 1)
            pe.wait_ge(lru_step, 12 * 8 * DEPTH)
            pe.wait_ge(y_rs, 4 * DEPTH)
            pe.transpose(PX[:, 0, 0:P], last[:].rearrange("p l r k -> p (l r k)"), ident[:]).then_inc(last_turned, 1)
            for half in range(2):
                pe.wait_ge(x_new, 16 * DEPTH + 4 * half + 4)
                for grp in range(5):
                    b = 5 * half + grp
                    if b == 4:
                        pe.wait_ge(last_placed, 1)
                    if b >= 8:
                        pe.wait_ge(out_placed[0], b - 7)
                    for k in range(4):
                        mm = pe.transpose(out_bank(b)[:, P * k:P * k + P], X[:, 4 * half + k, cols(grp)], ident[:])
                    mm.then_inc(out_turned, 1)

        @block.scalar
        def _(act):
            def split_hi(n, first=False):
                act.wait_ge(w_landed[n.slot], 4 * (n.value - n.slot) + 16)
                need(act, tile_done, n.value - 1, first=first)
                act.activation(w_hi[:, n.slot % 2, :, :], w_raw[:, n.slot, :, :], ACT.Copy).then_inc(w_hi_ready, 1)

            def input_tile(l, s, k):
                S = 2 * l + s
                act.wait_ge(x_new, 8 * S + k + 1)
                act.activation(h_hi[:, k, :], X[:, k, :], ACT.Copy, scale=gain(k, R_MPRE if s else R_GPRE)).then_inc(h_hi_ready, 1)

            def x_square(l, s, k):
                S = 2 * l + s
                if k == 0:
                    need(act, x_ssq, S, first=s == 0)
                    act.activation(acc_x[:], X[:, k, :], ACT.Square).then_inc(x_squared, 1)
                else:
                    if k > 2:
                        act.wait_ge(x_summed, 7 * S + k - 2)
                    act.activation(sq[:, k % 2, :], X[:, k, :], ACT.Square).then_inc(x_squared, 1)

            def y_square(l, s, k, odd=None):
                Y_ = 2 * l + s
                if s == 1:
                    act.wait_ge(f_scaled, 8 * l + k + 1)
                if isinstance(k, int) and k == 0:
                    need(act, y_ssq, Y_, first=s == 0)
                    act.activation(acc_y[:], Y[:, k, :], ACT.Square).then_inc(y_squared, 1)
                else:
                    if not isinstance(k, int):
                        act.wait_ge(y_summed, 7 * Y_ + k - 2)
                        own_wait(act)
                    elif k > 2:
                        act.wait_ge(y_summed, 7 * Y_ + k - 2)
                    act.activation(sq[:, (k if odd is None else odd) % 2, :], Y[:, k, :], ACT.Square).then_inc(y_squared, 1)

            def load_table(func):
                act.activation(warm[:], eps_col[:], func)

            def inverse_rms(dst, ssq, value, done, count, power):
                act.wait_ge(ssq, value)
                act.activation(halves(dst), PX[:, 0:2, 0:HT], ACT.Ln, scale=1.0 / (KT * P), bias=eps_col[:, 0:1]).then_inc(done, 1)
                act.wait_ge(done, count + 1)
                act.activation(dst, dst, ACT.Exp, scale=power).then_inc(done, 1)

            def qk_split(l, p, i):
                g = 4 * l + p
                act.wait_ge(evacuated, TL * l + 12 * p + i + 1)
                act.activation(qk_hi[:, i, :], T[:, i % 2, :], ACT.Copy).then_inc(qk_hi_ready, 1)

            def stage_k(l, p, m):
                g = 4 * l + p
                act.wait_ge(k_turned, 2 * g + m + 1)
                need(act, stored[m], 32 * 2 * g, first=p == 0)
                if m == 0:
                    need(act, pv_done, 10 * g, first=p == 0)
                act.activation(stage[0:NS, m, 0, :], PX[0:NS, 1, 0:P], ACT.Copy)
                act.activation(stage[:, m, 1:5, :], PX[:, 0, :].rearrange("p (g c) -> p g c", c=P), ACT.Copy).then_inc(k_staged, 1)

            def v_split(l, p, u):
                g = 4 * l + p
                act.wait_ge(evacuated, TL * l + 12 * p + 4 + u + 1)
                act.activation(v_hi[:, :, u, :], stage[:, u, :, :], ACT.Copy).then_inc(v_hi_ready, 1)

            def past_split(l, p):
                g = 4 * l + p
                act.wait_ge(past_turned, g + 1)
                act.activation(pk_hi[:], PX[:, 2, :].rearrange("p (m c) -> p m c", m=2), ACT.Copy).then_inc(pk_hi_ready, 1)
                act.activation(pv_hi[:], pv_raw[:], ACT.Copy).then_inc(pv_hi_ready, 1)

            def exponents(l, p, s):
                sg, qs = 10 * (4 * l + p) + s, s % 5
                nr, w, b = (NS, NKS, s % 2) if qs == 0 else (P, P * qs, s % 2)
                act.wait_ge(max_ready, sg + 1)
                for m in range(2):
                    buf = s1[0:nr, s % 3, 0:w] if m == 0 else s2[0:nr, b, 0:w]
                    act.activation(buf, buf, ACT.Exp, bias=neg_mx[0:nr, b, m:m + 1], scale=SCALE,
                                   accum_out=lsum[0:nr, b, m:m + 1]).then_inc(exp_done, 1)

            def p_split(l, p, s):
                sg, qs = 10 * (4 * l + p) + s, s % 5
                act.wait_ge(p_turned, sg + 1)
                need(act, pv_done, sg, first=p + s == 0)
                nk, w = (3, NS) if qs == 0 else (qs, P)
                act.activation(pt_hi[:, 0:nk, 0:w], PX[:, 2, 0:P * nk].rearrange("p (k c) -> p k c", c=P)[:, :, 0:w], ACT.Copy).then_inc(pt_hi_ready, 1)

            def place_o(l, p, s):
                sg, u, qs = 10 * (4 * l + p) + s, s // 5, s % 5
                act.wait_ge(pv_done, sg + 1)
                w, c = (NS, slice(0, NS)) if qs == 0 else (P, cols(qs))
                act.activation(O[:, 2 * p + u, c], PX[:, 3, 0:w], ACT.Copy).then_inc(o_placed, 1)

            def gelu(l, p, u):
                act.wait_ge(evacuated, TL * l + 12 * p + 8 + u + 1)
                act.activation(L[:, 2 * p + u, :], T[:, u, :], ACT.Gelu_apprx_tanh).then_inc(gelu_done, 1)

            def gate_a(l, p, u):
                act.wait_ge(evacuated, TL * l + 12 * p + 10 + u + 1)
                act.activation(GA[:, 2 * p + u, :], T[:, u, :], ACT.Tanh, scale=0.5).then_inc(ga_done, 1)

            def conv_start(l, p, u):
                g2 = 2 * (4 * l + p) + u
                f = 2 * p + u
                act.wait_ge(evacuated, TL * l + 12 * p + 6 + u + 1)
                need(act, lru_step, 12 * g2 if u == 0 else 12 * g2 - 9, first=p + u == 0)
                act.activation(uc[:], U[:, u, 0:LW], ACT.Identity, scale=gain(f, R_CW), bias=gain(f, R_CB)).then_inc(conv_first, 1)

            def gate_acts(l, p, u):
                g2 = 2 * (4 * l + p) + u
                f = 2 * p + u
                act.wait_ge(gates_done, g2 + 1)
                need(act, lru_step, 12 * g2, first=p + u == 0)
                need(act, pv_lo_ready, 4 * l + p + 2 if p < 3 else 0)
                for j, t in enumerate((tr, ti)):
                    act.activation(t[:].rearrange("p (a b) -> p a b", a=2), PX[:, 2 * j:2 * j + 2, 0:LH], ACT.Tanh, scale=0.5,
                                   bias=par[:, f, R_BR + j:R_BR + j + 1]).then_inc(lru_act, 1)
                act.wait_ge(lru_act, 5 * g2 + 1)
                act.activation(aa[:], tr[:], ACT.Exp, scale=gain(f, R_LAM), bias=gain(f, R_LAM)).then_inc(lru_act, 1)
                act.wait_ge(lru_act, 5 * g2 + 3)
                act.activation(tr[:], tr[:], ACT.Tanh, scale=gain(f, R_LAM), bias=gain(f, R_LAM)).then_inc(lru_act, 1)

            def lru_root(l, p, u):
                g2 = 2 * (4 * l + p) + u
                act.wait_ge(lru_step, 12 * g2 + 2)
                act.activation(tm[:], tm[:], ACT.Sqrt, scale=-1.0).then_inc(lru_act, 1)

            def sub_square(l, p, u):
                g2 = 2 * (4 * l + p) + u
                act.wait_ge(o_placed, 10 * (4 * l + p) + 5 * u + 5)
                act.wait_ge(pv_done, 10 * (4 * l + p) + 10)
                need(act, o_ssq, g2, first=p + u == 0)
                act.activation(sq_o[:], O[:, 2 * p + u, :], ACT.Square).then_inc(o_squared, 1)

            def sub_rs(l, p, u):
                g2 = 2 * (4 * l + p) + u
                act.wait_ge(o_ssq, g2 + 1)
                need(act, o_normed, g2, first=p + u == 0)
                act.activation(halves(rr[:]), PX[:, 2:4, 0:HT], ACT.Ln, scale=1.0 / VD, bias=eps_col[:, 0:1]).then_inc(o_rs, 1)
                act.wait_ge(o_rs, 2 * g2 + 1)
                act.activation(rr[:], rr[:], ACT.Exp, scale=-0.5).then_inc(o_rs, 1)

            def up_four(l, c, r):
                for j in range(4):
                    n, i = mlp_tile(l, c, 4 * r, j), 4 * r + j
                    if isinstance(r, int) and c == 0 and j < 2:
                        if j == 0:
                            split_hi(n + 2)
                    else:
                        split_hi(n + 1)
                    act.wait_ge(evacuated, n.value + 1)
                    act.activation(T[:, j % 2, :], T[:, j % 2, :], ACT.Square).then_inc(relu2_done, 1)
                    act.wait_ge(relu2_done, 16 * (2 * l + c) + i + 1)
                    if not isinstance(r, int):
                        own_wait(act)
                    act.activation(u_hi[:, i, :], T[:, j % 2, :], ACT.Copy).then_inc(u_hi_ready, 1)
                    if isinstance(r, int) and c == 0:
                        for k in ((), (0, 1, 2), (3, 4, 5), (6, 7))[j]:
                            x_square(l, 1, k)

            def down_four(l, c, r):
                for m in range(2):
                    for half in range(2):
                        if not (isinstance(r, int) and r + c + m + half == 6):
                            split_hi(mlp_tile(l, c, 16 + 4 * r, 2 * m + half) + 1)
                    if c == 1:
                        y_square(l, 1, 2 * r + m, m)

            for row, name in ((R_GPRE, "g_mix_pre"), (R_GPOST, "g_mix_post"), (R_MPRE, "g_mlp_pre"), (R_MPOST, "g_mlp_post"),
                              (R_CB, "conv_b"), (R_BR, "b_rg"), (R_BI, "b_ig"), (R_LAM, "lru_lambda"), (R_SL, "state_lru")):
                act.dma_start(rows[row:row + 16 * (DEPTH - 1) + 1:16, :], A[name].rearrange("l o d -> (l o) d") if name == "state_lru" else A[name]).then_inc(par_landed, 16)
            for l in range(DEPTH):
                act.dma_start(rows[16 * l + R_CW:16 * l + R_CW + 4, :], A["conv_w"][l]).then_inc(par_landed, 16)
                act.dma_start(rows[16 * l + R_SC:16 * l + R_SC + 3, :], A["state_conv"][l, 0]).then_inc(par_landed, 16)
            act.wait_ge(par_step, 2)
            act.activation(lsc[:, 1, :], lsc[:, 0, :], ACT.Exp, scale=-1.0).then_inc(lam_act, 1)
            act.wait_ge(lam_step, 4)
            act.activation(lsc[:, 7, 0:4], lsc[:, 6, 0:4], ACT.Exp).then_inc(lam_act, 1)
            for k in range(KT):
                act.wait_ge(x_turned, k + 1)
                c = NS + 2 * P
                act.activation(X[:, k, 0:c], PJ[:, k % 2, 0, 0:c], ACT.Copy)
                act.activation(X[:, k, c:NT], PJ[:, k % 2, 1, 0:2 * P], ACT.Copy).then_inc(x_new, 1)
            act.wait_ge(par_step, 1)

            with act.Fori(0, DEPTH) as l:
                N = TileNo(TL * l, 0)
                for i in range(2):
                    split_hi(N + i, first=True)
                for k in range(KT):
                    input_tile(l, 0, k)
                    x_square(l, 0, k)
                load_table(ACT.Ln)
                for p in range(4):
                    n = N + 12 * p
                    for i in range(6):
                        if not (p == 0 and i == 0):
                            split_hi(n + (i + 1))
                        if p == 0 and i == 0:
                            inverse_rms(rs[:], x_ssq, 2 * l + 1, x_rs, 4 * l, -0.5)
                        if i == 2 and p > 0:
                            gate_acts(l, p - 1, 0)
                            conv_start(l, p - 1, 1)
                            lru_root(l, p - 1, 0)
                        if i == 3 and p > 0:
                            sub_rs(l, p - 1, 0)
                        if i == 3:
                            stage_k(l, p, 0)
                        if i < 4:
                            qk_split(l, p, i)
                        if i == 0 and p > 0:
                            place_o(l, p - 1, 9)
                            past_split(l, p)
                            sub_square(l, p - 1, 0)
                            load_table(ACT.Exp)
                        if i == 3 and p > 0:
                            sub_square(l, p - 1, 1)
                        if i == 4:
                            if p > 0:
                                gate_acts(l, p - 1, 1)
                                lru_root(l, p - 1, 1)
                            v_split(l, p, 0)
                            stage_k(l, p, 1)
                            if p == 0:
                                past_split(l, p)
                        if i == 5:
                            if p > 0:
                                sub_rs(l, p - 1, 1)
                            v_split(l, p, 1)
                    for j in range(12):
                        if j % 2 == 0:
                            split_hi(n + (7 + j // 2))
                        if 3 <= j:
                            place_o(l, p, j - 3)
                        if 2 <= j:
                            p_split(l, p, j - 2)
                        if j < 10:
                            exponents(l, p, j)
                        if j == 10:
                            gelu(l, p, 0)
                            gelu(l, p, 1)
                        if j == 11:
                            gate_a(l, p, 0)
                            gate_a(l, p, 1)
                        if j == 6:
                            conv_start(l, p, 0)
                for i in range(8):
                    n = N + (T_GB + i)
                    split_hi(n + 1)
                    if i == 2:
                        gate_acts(l, 3, 0)
                        conv_start(l, 3, 1)
                        lru_root(l, 3, 0)
                    if i == 5:
                        gate_acts(l, 3, 1)
                        lru_root(l, 3, 1)
                    if i == 3:
                        sub_rs(l, 3, 0)
                    act.wait_ge(evacuated, n.value + 1)
                    act.activation(GB[:, i, :], T[:, i % 2, :], ACT.Tanh, scale=0.5).then_inc(gb_done, 1)
                    if i == 0:
                        place_o(l, 3, 9)
                        sub_square(l, 3, 0)
                        load_table(ACT.Exp)
                    if i == 4:
                        sub_square(l, 3, 1)
                    if i == 6:
                        sub_rs(l, 3, 1)
                    for f in o_turns[i]:
                        act.wait_ge(o_normed, 8 * l + f + 1)
                        act.activation(o_hi[:, f, :], O[:, f, :], ACT.Copy).then_inc(o_hi_ready, 1)
                with act.Fori(0, KT // 4) as r:
                    for j in range(4):
                        n, i = mixer_tile(l, T_WA, r, j), 4 * r + j
                        split_hi(n + 1)
                        if j == 0:
                            act.wait_ge(tile_done, TL * l + T_WA)
                        act.wait_ge(lru_step, 12 * (8 * l + i + 1))
                        own_wait(act)
                        act.activation(l_hi[:, i, :], L[:, i, :], ACT.Copy).then_inc(l_hi_ready, 1)
                with act.Fori(0, KT // 4) as r:
                    for j in range(4):
                        n, i = mixer_tile(l, T_WL, r, j), 4 * r + j
                        split_hi(n + 1)
                        act.wait_ge(b_scaled, 8 * l + i + 1)
                        own_wait(act)
                        act.activation(m_hi[:, i, :], GB[:, i, :], ACT.Copy).then_inc(m_hi_ready, 1)
                for i in range(8):
                    n = N + (T_WO + i)
                    split_hi(n + 1)
                    if i == 7:
                        load_table(ACT.Ln)
                    act.wait_ge(evacuated, n.value + 1)
                    y_square(l, 0, i)
                split_hi(N + (T_MLP + 1))
                inverse_rms(rn[:], y_ssq, 2 * l + 1, y_rs, 4 * l, -0.5)
                for k in range(KT):
                    input_tile(l, 1, k)
                for c in range(2):
                    up_four(l, c, 0)
                    with act.Fori(1, 4) as r:
                        up_four(l, c, r)
                    if c == 0:
                        inverse_rms(r2q[:], x_ssq, 2 * l + 2, x_rs, 4 * l + 2, -1.0)
                    down_four(l, c, 0)
                    with act.Fori(1, 3) as r:
                        down_four(l, c, r)
                    down_four(l, c, 3)
                inverse_rms(rn[:], y_ssq, 2 * l + 2, y_rs, 4 * l + 2, -0.5)
            act.wait_ge(last_turned, 1)
            act.activation(last_t[:], PX[:, 0, 0:P], ACT.Copy).then_inc(last_placed, 1)
            for grp in range(5):
                nr = NS if grp == 0 else P
                act.wait_ge(out_turned, grp + 1)
                act.activation(y_out[0:nr, grp, 0, :], out_bank(grp)[0:nr, :], ACT.Copy).then_inc(out_placed[0], 1)

        @block.vector
        def _(dve):
            def split_lo(n):
                dve.wait_ge(w_hi_ready, n.value + 1)
                dve.tensor_tensor(w_lo[:, n.slot, :, :], w_raw[:, n.slot, :, :], w_hi[:, n.slot % 2, :, :].bitcast(F32), ALU.subtract).then_inc(w_lo_ready, 1)

            def input_tile(l, s, k):
                S = 2 * l + s
                dve.wait_ge(h_hi_ready, 8 * S + k + 1)
                dve.scalar_tensor_tensor(out=h_lo[:, k, :], in0=X[:, k, :], scalar=gain(k, R_MPRE if s else R_GPRE),
                                         in1=h_hi[:, k, :].bitcast(F32), op0=ALU.mult, op1=ALU.subtract).then_inc(h_lo_ready, 1)

            def x_sum(l, s, k):
                S = 2 * l + s
                if k > 0:
                    dve.wait_ge(x_squared, 8 * S + k + 1)
                    if k > 1:
                        dve.wait_ge(x_summed, 7 * S + k - 1)
                    dve.tensor_tensor(acc_x[:], acc_x[:], sq[:, k % 2, :], ALU.add).then_inc(x_summed, 1)

            def y_sum(l, s, k, odd=None):
                Y_ = 2 * l + s
                dve.wait_ge(y_squared, 8 * Y_ + k + 1)
                if not isinstance(k, int) or k > 1:
                    dve.wait_ge(y_summed, 7 * Y_ + k - 1)
                dve.tensor_tensor(acc_y[:], acc_y[:], sq[:, (k if odd is None else odd) % 2, :], ALU.add).then_inc(y_summed, 1)

            def update_x(l, s):
                Y_ = 2 * l + s
                dve.wait_ge(y_rs, 4 * l + 2 * s + 2)
                lag = 3
                for k in range(KT + lag if s == 0 else KT):
                    if k < KT:
                        dve.scalar_tensor_tensor(out=Y[:, k, :], in0=Y[:, k, :], scalar=gain(k, R_MPOST if s else R_GPOST),
                                                 in1=rn[:], op0=ALU.mult, op1=ALU.mult).then_inc(y_scaled, 1)
                    if s == 0 and k >= lag:
                        input_tile(l, 1, k - lag)

            def next_parameters(first, end):
                for later in range(1, DEPTH):
                    dve.tensor_copy(par[:, :, 16 * (later - 1) + first:16 * (later - 1) + end], par[:, :, 16 * later + first:16 * later + end])

            def times_rs(dst, n):
                dve.wait_ge(tile_done, n.value + 1)
                dve.tensor_tensor(halves(dst), proj(n), halves(rs[:]), ALU.mult).then_inc(evacuated, 1)

            def qk_tile(l, p, i):
                g = 4 * l + p
                if i < 2:
                    need(dve, ga_done, 2 * g - 1 + i, first=p == 0)
                else:
                    dve.wait_ge(qk_lo_ready, 4 * g + i - 1)
                times_rs(T[:, i % 2, :], TileNo(TL * l, 0) + (12 * p + i))

            def v_rows(l, p, u):
                g = 4 * l + p
                n = TileNo(TL * l, 0) + 12 * p + 4 + u
                dve.wait_ge(tile_done, n.value + 1)
                dve.wait_ge(stored[u], 32 * (2 * g + 1))
                for grp in range(5):
                    src = PJ[:, n.slot % 2, 1, 0:P] if grp == 0 else PJ[:, n.slot % 2, 0, P * (grp - 1):P * grp]
                    i = dve.tensor_scalar(stage[:, u, grp, :], src, rs_tok[:, grp:grp + 1], None, ALU.mult)
                i.then_inc(evacuated, 1)

            def u_tile(l, p, u):
                g2 = 2 * (4 * l + p) + u
                n = TileNo(TL * l, 0) + (12 * p + 6 + u)
                f = 2 * p + u
                dve.tensor_copy(U[:, u, 0:3], par[:, f, R_SC:R_SC + 3])
                dve.memset(U[:, u, PR:PR + 3], 0.0)
                dve.memset(U[:, u, 550:552], 0.0)
                dve.wait_ge(tile_done, n.value + 1)
                dve.tensor_tensor(U[:, u, 3:3 + NS], PJ[:, n.slot % 2, 0, 0:NS], rs[:, 0:NS], ALU.mult)
                dve.tensor_tensor(U[:, u, 38:38 + HT - NS], PJ[:, n.slot % 2, 0, NS:HT], rs[:, NS:HT], ALU.mult)
                dve.tensor_tensor(U[:, u, 38 + HT - NS:38 + NP_], PJ[:, n.slot % 2, 1, 0:HT], rs[:, HT:NT], ALU.mult).then_inc(evacuated, 1)

            def gated_tile(l, p, i):
                g = 4 * l + p
                if i < 2:
                    dve.wait_ge(k_turned, 2 * g + i + 1)
                    dve.wait_ge(qk_lo_ready, 4 * g + 3 + i)
                else:
                    dve.wait_ge(gelu_done, 2 * g + i - 1)
                times_rs(T[:, i % 2, :], TileNo(TL * l, 0) + (12 * p + 8 + i))

            def head_bias(l, p, u):
                h = 2 * p + u
                slope = 2.0 ** (-8.0 * (h + 1) / NHEAD)
                g2 = 2 * (4 * l + p) + u
                need(dve, biased, 10 * g2, first=p + u == 0)
                dve.tensor_scalar(bias_s[:], dist_s[:], -slope / SCALE, None, ALU.mult).then_inc(bias_ready, 1)
                dve.tensor_scalar(bias_p[:], dist_p[:], -slope / SCALE, None, ALU.mult).then_inc(bias_ready, 1)

            def bias_max(l, p, s):
                g = 4 * l + p
                sg, u, qs = 10 * g + s, s // 5, s % 5
                nr, w, b = (NS, NKS, s % 2) if qs == 0 else (P, P * qs, s % 2)
                if qs == 0:
                    dve.wait_ge(bias_ready, 2 * (2 * g + u) + 2)
                if s == 0:
                    dve.wait_ge(stored[0], 32 * (2 * g + 2))
                    dve.wait_ge(stored[1], 32 * (2 * g + 2))
                    dve.wait_ge(v_lo_ready, 2 * g + 2)
                if s >= 3:
                    dve.wait_ge(p_turned, sg - 2)
                need(dve, p_ready, sg - 1, first=p == 0 and s < 2)
                dve.wait_ge(scores_done, sg + 1)
                own_wait(dve)
                bias = bias_s[:] if qs == 0 else bias_p[:, NP_ - w:NP_]
                for m in range(2):
                    dve.tensor_tensor_reduce(out=s1[0:nr, s % 3, 0:w] if m == 0 else s2[0:nr, b, 0:w], in0=PX[0:nr, m, 0:w], in1=bias,
                                             scale=1.0, scalar=-3.0e38, op0=ALU.add, op1=ALU.max,
                                             accum_out=mx[0:nr, b, m:m + 1]).then_inc(biased, 1)
                dve.wait_ge(biased, 2 * sg + 2)
                dve.tensor_scalar(neg_mx[0:nr, b, :], mx[0:nr, b, :], -SCALE, None, ALU.mult).then_inc(max_ready, 1)

            def combine(l, p, s):
                sg, qs = 10 * (4 * l + p) + s, s % 5
                nr, w, b = (NS, NKS, s % 2) if qs == 0 else (P, P * qs, s % 2)
                p1 = s1[0:nr, s % 3, 0:w]
                dve.wait_ge(exp_done, 2 * sg + 2)
                dve.reciprocal(rl[0:nr, b, :], lsum[0:nr, b, :]).then_inc(norm_step, 1)
                dve.wait_ge(norm_step, 3 * sg + 1)
                dve.tensor_tensor(rl2[0:nr, b:b + 1], rl[0:nr, b, 1:2], neg_lam[0:nr, 0:1], ALU.mult).then_inc(norm_step, 1)
                dve.tensor_scalar(p1, p1, rl[0:nr, b, 0:1], None, ALU.mult).then_inc(norm_step, 1)
                dve.wait_ge(norm_step, 3 * sg + 3)
                dve.scalar_tensor_tensor(out=p1, in0=s2[0:nr, b, 0:w], scalar=rl2[0:nr, b:b + 1], in1=p1,
                                         op0=ALU.mult, op1=ALU.add).then_inc(p_ready, 1)

            def p_split(l, p, s):
                sg, qs = 10 * (4 * l + p) + s, s % 5
                nk, w = (3, NS) if qs == 0 else (qs, P)
                dve.wait_ge(pt_hi_ready, sg + 1)
                dve.tensor_tensor(pt_lo[:, 0:nk, 0:w], PX[:, 2, 0:P * nk].rearrange("p (k c) -> p k c", c=P)[:, :, 0:w],
                                  pt_hi[:, 0:nk, 0:w].bitcast(F32), ALU.subtract).then_inc(pt_lo_ready, 1)

            def past_lo(l, p):
                dve.wait_ge(pk_hi_ready, 4 * l + p + 1)
                dve.tensor_tensor(pk_lo[:], PX[:, 2, :].rearrange("p (m c) -> p m c", m=2), pk_hi[:].bitcast(F32), ALU.subtract).then_inc(pk_lo_ready, 1)

            def conv(l, p, u):
                g2, f = 2 * (4 * l + p) + u, 2 * p + u
                dve.wait_ge(conv_first, g2 + 1)
                for j in range(1, CW):
                    if j > 1:
                        dve.wait_ge(conv_step, 3 * g2 + j - 1)
                    dve.scalar_tensor_tensor(out=uc[:], in0=U[:, u, j:j + LW], scalar=gain(f, R_CW + j), in1=uc[:],
                                             op0=ALU.mult, op1=ALU.add).then_inc(conv_step, 1)

            def lru_a(l, p, u):
                g2 = 2 * (4 * l + p) + u
                need(dve, lru_step, 12 * g2, first=p + u == 0)
                dve.wait_ge(lru_act, 5 * g2 + 3)
                dve.tensor_tensor(tm[:], aa[:], aa[:], ALU.mult).then_inc(lru_step, 1)
                dve.wait_ge(lru_act, 5 * g2 + 4)
                dve.wait_ge(lru_step, 12 * g2 + 1)
                dve.scalar_tensor_tensor(out=tm[:], in0=tm[:], scalar=1.0, in1=tr[:], op0=ALU.add, op1=ALU.mult).then_inc(lru_step, 1)
                dve.scalar_tensor_tensor(out=ti[:], in0=ti[:], scalar=1.0, in1=uc[:], op0=ALU.add, op1=ALU.mult).then_inc(lru_step, 1)

            def lru_b(l, p, u):
                g2, f = 2 * (4 * l + p) + u, 2 * p + u
                dve.wait_ge(lru_act, 5 * g2 + 5)
                dve.wait_ge(lru_step, 12 * g2 + 3)
                dve.scalar_tensor_tensor(out=ti[:], in0=ti[:], scalar=0.5, in1=tm[:], op0=ALU.mult, op1=ALU.mult).then_inc(lru_step, 1)
                dve.wait_ge(lru_step, 12 * g2 + 4)
                dve.tensor_tensor_scan(tm[:, 0:NS], aa[:, 0:NS], ti[:, 0:NS], gain(f, R_SL), ALU.mult, ALU.add).then_inc(lru_step, 1)
                dve.tensor_tensor_scan(tm[:, PR:PR + NP_], aa[:, PR:PR + NP_], ti[:, PR:PR + NP_], 0.0, ALU.mult, ALU.add).then_inc(lru_step, 1)
                dve.wait_ge(gelu_done, g2 + 1)
                dve.wait_ge(lru_step, 12 * g2 + 6)
                dve.tensor_tensor(L[:, f, 0:NS], L[:, f, 0:NS], tm[:, 0:NS], ALU.mult).then_inc(lru_step, 1)
                dve.tensor_tensor(L[:, f, NS:NT], L[:, f, NS:NT], tm[:, PR:PR + NP_], ALU.mult).then_inc(lru_step, 1)
                dve.tensor_copy(last[:, l, 0:3, f], U[:, u, 547:550]).then_inc(lru_step, 1)
                dve.tensor_copy(last[:, l, 3:6, f], U[:, u, NS:NS + 3]).then_inc(lru_step, 1)
                dve.tensor_copy(last[:, l, 6:7, f], tm[:, PR + NP_ - 1:PR + NP_]).then_inc(lru_step, 1)
                dve.tensor_copy(last[:, l, 7:8, f], tm[:, NS - 1:NS]).then_inc(lru_step, 1)

            def sub_norm(l, p, u):
                g2 = 2 * (4 * l + p) + u
                f = 2 * p + u
                dve.wait_ge(o_rs, 2 * g2 + 2)
                dve.scalar_tensor_tensor(out=O[:, f, :], in0=O[:, f, :], scalar=gs[:, 0:1], in1=rr[:], op0=ALU.mult, op1=ALU.mult).then_inc(o_normed, 1)

            def up_four(l, c, r):
                first = isinstance(r, int)
                for j in range(4):
                    n = mlp_tile(l, c, 4 * r, j)
                    if not (first and c == 0 and j < 2):
                        split_lo(n + 1)
                    if first and c == 0 and j < 2:
                        dve.wait_ge(gb_done, 8 * (l + 1))
                    else:
                        dve.wait_ge(u_lo_ready, 16 * (2 * l + c) + 4 * r + j - 1)
                    dve.wait_ge(tile_done, n.value + 1)
                    dve.tensor_scalar(halves(T[:, j % 2, :]), proj(n), 0.0, None, ALU.max).then_inc(evacuated, 1)
                    if first and c == 0:
                        if j == 0:
                            split_lo(n + 2)
                        for k in ((), (1,), (2, 3, 4), (5, 6, 7))[j]:
                            x_sum(l, 1, k)

            def down_four(l, c, r):
                for j in range(2):
                    m, n = 2 * r + j, mlp_tile(l, c, 16 + 4 * r, 2 * j)
                    for half in range(2):
                        if not (isinstance(r, int) and r + c + j + half == 6):
                            split_lo(n + (half + 1))
                    dve.wait_ge(tile_done, n.value + 2)
                    for half in range(2):
                        cl = slice(HT * half, HT * half + HT)
                        if c == 0:
                            if not isinstance(r, int) and half == 0:
                                own_wait(dve)
                            dve.tensor_copy(Y[:, m, cl], PJ[:, j, half, 0:HT]).then_inc(evacuated, 1)
                        else:
                            dve.tensor_tensor(Y[:, m, cl], Y[:, m, cl], PJ[:, j, half, 0:HT], ALU.add).then_inc(evacuated, 1)
                    if c == 1:
                        dve.wait_ge(evacuated, n.value + 2)
                        if isinstance(r, int) and r + j == 0:
                            dve.wait_ge(x_rs, 4 * l + 4)
                        dve.tensor_tensor(Y[:, m, :], Y[:, m, :], r2q[:], ALU.mult).then_inc(f_scaled, 1)
                        if not isinstance(r, int) or 2 * r + j > 1:
                            y_sum(l, 1, m - 1, 1 - j)

            dve.memset(ones[:], 1.0)
            dve.memset(eps_col[:], EPS)
            dve.memset(s1[:], 0.0)
            dve.wait_ge(const_step, 3)
            lam_init = [0.8 - 0.6 * math.exp(-0.3 * l) for l in range(DEPTH)]
            dve.tensor_scalar(bias_p[:], dist_p[:], -1.0, None, ALU.mult).then_inc(lam_step, 1)
            dve.tensor_scalar(bias_s[:], dist_s[:], -1.0, None, ALU.mult).then_inc(lam_step, 1)
            dve.wait_ge(lam_step, 2)
            dve.tensor_tensor(dist_p[:], dist_p[:], bias_p[:], ALU.max).then_inc(lam_step, 1)
            dve.wait_ge(lam_step, 3)
            dve.tensor_tensor(dist_s[:], dist_s[:], bias_s[:], ALU.max)
            dve.memset(dist_p[0:CHUNK, NP_ - CHUNK:NP_], NEG_DIST)
            dve.wait_ge(lam_landed, 16 * 5 * DEPTH)
            for l in range(DEPTH):
                for j in range(2):
                    i = dve.tensor_tensor_reduce(out=lprod[:], in0=lq[:, l, 2 * j, :], in1=lq[:, l, 2 * j + 1, :], scale=1.0, scalar=0.0,
                                                 op0=ALU.mult, op1=ALU.add, accum_out=lsc[:, 6, 2 * l + j:2 * l + j + 1])
                    if l == DEPTH - 1 and j == 1:
                        i.then_inc(lam_step, 1)
                    else:
                        i.then_inc(lambda_chain, 1)
                        dve.wait_ge(lambda_chain, 2 * l + j + 1)
            for l in range(DEPTH):
                dve.tensor_scalar(gs[:, l:l + 1], gs[:, l:l + 1], 1.0 - lam_init[l], None, ALU.mult)
            dve.wait_ge(par_turned, 1)
            dve.tensor_copy(par[:], PX[:, 0, 0:256].rearrange("p (k r) -> p k r", r=32)).then_inc(par_step, 1)
            dve.wait_ge(par_step, 1)
            for l in range(DEPTH):
                dve.tensor_scalar(par[:, :, 16 * l + R_BR:16 * l + R_BR + 2], par[:, :, 16 * l + R_BR:16 * l + R_BR + 2], 0.5, None, ALU.mult)
            zl = [par[:, :, 16 * l + R_LAM] for l in range(DEPTH)]
            step = [0]

            def link(ins):
                step[0] += 1
                ins.then_inc(param_chain, 1)
                dve.wait_ge(param_chain, step[0])

            for l in range(DEPTH):
                i = dve.tensor_scalar(lsc[:, 2, KT * l:KT * l + KT], zl[l], -1.0, None, ALU.mult)
            link(i)
            for l in range(DEPTH):
                i = dve.tensor_tensor(lsc[:, 0, KT * l:KT * l + KT], lsc[:, 2, KT * l:KT * l + KT], zl[l], ALU.max)
            link(i)
            dve.tensor_scalar(lsc[:, 2, :], lsc[:, 2, :], 0.0, None, ALU.max).then_inc(par_step, 1)
            dve.wait_ge(lam_act, 1)
            link(dve.tensor_scalar(lsc[:, 3, :], lsc[:, 1, :], 2.0, None, ALU.add))
            link(dve.reciprocal(lsc[:, 3, :], lsc[:, 3, :]))
            link(dve.tensor_tensor(lsc[:, 3, :], lsc[:, 3, :], lsc[:, 1, :], ALU.mult))
            link(dve.tensor_tensor(lsc[:, 4, :], lsc[:, 3, :], lsc[:, 3, :], ALU.mult))
            terms = 9
            link(dve.tensor_scalar(lsc[:, 5, :], lsc[:, 4, :], 1.0 / (2 * terms - 1), None, ALU.mult))
            for t in range(terms - 2, 0, -1):
                link(dve.scalar_tensor_tensor(out=lsc[:, 5, :], in0=lsc[:, 5, :], scalar=1.0 / (2 * t + 1), in1=lsc[:, 4, :],
                                              op0=ALU.add, op1=ALU.mult))
            link(dve.scalar_tensor_tensor(out=lsc[:, 5, :], in0=lsc[:, 5, :], scalar=1.0, in1=lsc[:, 3, :], op0=ALU.add, op1=ALU.mult))
            link(dve.scalar_tensor_tensor(out=lsc[:, 5, :], in0=lsc[:, 5, :], scalar=2.0, in1=lsc[:, 2, :], op0=ALU.mult, op1=ALU.add))
            for l in range(DEPTH):
                link(dve.tensor_scalar(zl[l], lsc[:, 5, KT * l:KT * l + KT], -4.0, None, ALU.mult))
            dve.wait_ge(lam_act, 2)
            for l in range(DEPTH):
                link(dve.tensor_tensor(neg_lam[:, l:l + 1], lsc[:, 7, 2 * l + 1:2 * l + 2], lsc[:, 7, 2 * l:2 * l + 1], ALU.subtract))
                link(dve.tensor_scalar(neg_lam[:, l:l + 1], neg_lam[:, l:l + 1], -lam_init[l], None, ALU.add))

            with dve.Fori(0, DEPTH) as l:
                N = TileNo(TL * l, 0)
                for i in range(2):
                    split_lo(N + i)
                for k in range(KT):
                    input_tile(l, 0, k)
                    if k > 1:
                        x_sum(l, 0, k - 1)
                x_sum(l, 0, KT - 1)
                for p in range(4):
                    n = N + 12 * p
                    for i in range(6):
                        if not (p == 0 and i == 0):
                            split_lo(n + (i + 1))
                        if p == 0 and i == 0:
                            dve.wait_ge(x_rs, 4 * l + 2)
                        if i == 2 and p > 0:
                            lru_a(l, p - 1, 0)
                        if i == 3 and p > 0:
                            conv(l, p - 1, 1)
                            lru_b(l, p - 1, 0)
                        if i < 4:
                            qk_tile(l, p, i)
                        if p == 0 and i == 0:
                            dve.wait_ge(rs_turned, l + 1)
                            dve.tensor_copy(rs_tok[:], PX[:, 3, 0:10].rearrange("p (g c) -> p g c", c=2)[:, :, 0]).then_inc(rs_tok_ready, 1)
                        if i == 0 and p > 0:
                            past_lo(l, p)
                        if i == 3 and p > 0:
                            sub_norm(l, p - 1, 0)
                        if i == 4:
                            if p == 0:
                                dve.wait_ge(rs_tok_ready, l + 1)
                            else:
                                lru_a(l, p - 1, 1)
                            v_rows(l, p, 0)
                        if i == 5:
                            if p == 0:
                                past_lo(l, p)
                            else:
                                lru_b(l, p - 1, 1)
                                sub_norm(l, p - 1, 1)
                            v_rows(l, p, 1)
                    for j in range(12):
                        if j % 2 == 0:
                            split_lo(n + (7 + j // 2))
                        if j in (0, 5):
                            head_bias(l, p, j // 5)
                        if j < 10:
                            bias_max(l, p, j)
                        if 1 <= j < 11:
                            combine(l, p, j - 1)
                        if 2 <= j:
                            p_split(l, p, j - 2)
                        if j in (1, 3):
                            u_tile(l, p, j // 2)
                        if j in (5, 7):
                            gated_tile(l, p, (j - 5) // 2)
                        if j >= 10:
                            gated_tile(l, p, j - 8)
                        if j == 10:
                            conv(l, p, 0)
                for i in range(8):
                    n = N + (T_GB + i)
                    split_lo(n + 1)
                    if i == 2:
                        lru_a(l, 3, 0)
                    if i < 2:
                        dve.wait_ge(ga_done, 2 * (4 * l + 3) + i + 1)
                    else:
                        dve.wait_ge(gb_done, 8 * l + i - 1)
                    times_rs(T[:, i % 2, :], n)
                    if i == 3:
                        conv(l, 3, 1)
                        lru_b(l, 3, 0)
                        sub_norm(l, 3, 0)
                    if i == 5:
                        lru_a(l, 3, 1)
                    if i == 6:
                        lru_b(l, 3, 1)
                        sub_norm(l, 3, 1)
                    for f in o_turns[i]:
                        dve.wait_ge(o_hi_ready, 8 * l + f + 1)
                        dve.tensor_tensor(o_lo[:, f, :], O[:, f, :], o_hi[:, f, :].bitcast(F32), ALU.subtract).then_inc(o_lo_ready, 1)
                with dve.Fori(0, KT // 4) as r:
                    for j in range(4):
                        n, i = mixer_tile(l, T_WA, r, j), 4 * r + j
                        split_lo(n + 1)
                        dve.wait_ge(l_hi_ready, 8 * l + i + 1)
                        dve.tensor_tensor(l_lo[:, i, :], L[:, i, :], l_hi[:, i, :].bitcast(F32), ALU.subtract).then_inc(l_lo_ready, 1)
                        dve.wait_ge(tile_done, n.value + 1)
                        dve.wait_ge(ga_done, 8 * (l + 1))
                        dve.scalar_tensor_tensor(out=halves(GA[:, i, :]), in0=halves(GA[:, i, :]), scalar=1.0, in1=proj(n),
                                                 op0=ALU.add, op1=ALU.mult).then_inc(evacuated, 1)
                with dve.Fori(0, KT // 4) as r:
                    for j in range(4):
                        n, i = mixer_tile(l, T_WL, r, j), 4 * r + j
                        split_lo(n + 1)
                        dve.wait_ge(tile_done, n.value + 1)
                        dve.wait_ge(gb_done, 8 * (l + 1))
                        dve.scalar_tensor_tensor(out=halves(GB[:, i, :]), in0=halves(GB[:, i, :]), scalar=1.0, in1=proj(n),
                                                 op0=ALU.add, op1=ALU.mult).then_inc(evacuated, 1)
                        dve.wait_ge(evacuated, n.value + 1)
                        dve.tensor_tensor(GB[:, i, :], GB[:, i, :], GA[:, i, :], ALU.add).then_inc(b_scaled, 1)
                for i in range(8):
                    n = N + (T_WO + i)
                    split_lo(n + 1)
                    dve.wait_ge(tile_done, n.value + 1)
                    dve.tensor_scalar(halves(Y[:, i, :]), proj(n), 0.5, None, ALU.mult).then_inc(evacuated, 1)
                    if i > 1:
                        y_sum(l, 0, i - 1)
                y_sum(l, 0, 7)
                split_lo(N + (T_MLP + 1))
                update_x(l, 0)
                dve.wait_ge(h_lo_ready, 16 * (l + 1))
                next_parameters(0, R_MPOST)
                next_parameters(R_MPOST + 1, 16)
                dve.tensor_copy(gs[:, 0:DEPTH - 1], gs[:, 1:DEPTH])
                dve.tensor_copy(neg_lam[:, 0:DEPTH - 1], neg_lam[:, 1:DEPTH])
                for c in range(2):
                    up_four(l, c, 0)
                    with dve.Fori(1, 4) as r:
                        up_four(l, c, r)
                    down_four(l, c, 0)
                    with dve.Fori(1, 3) as r:
                        down_four(l, c, r)
                    down_four(l, c, 3)
                y_sum(l, 1, 7)
                update_x(l, 1)
                dve.wait_ge(y_scaled, 8 * (2 * l + 2))
                next_parameters(R_MPOST, R_MPOST + 1)
            for grp in range(5):
                nr = NS if grp == 0 else P
                dve.wait_ge(out_turned, 5 + grp + 1)
                dve.tensor_copy(y_out[0:nr, grp, 1, :], out_bank(5 + grp)[0:nr, :]).then_inc(out_placed[1], 1)


_INS = ["x_prompt", "x_sample", "cache_k", "cache_v", "state_conv", "state_lru", "w_in", "lambda_q1", "lambda_k1", "lambda_q2",
        "lambda_k2", "g_sub", "conv_w", "conv_b", "w_rg", "b_rg", "w_ig", "b_ig", "lru_lambda", "w_branch_attn", "w_branch_lru",
        "w_out", "w_up", "w_down", "g_mix_pre", "g_mix_post", "g_mlp_pre", "g_mlp_post"]


def kernel(**inputs):
    import numpy as _np
    import concourse.bacc as _bacc
    from concourse import mybir as _mybir
    from concourse.bass_utils import run_bass_kernel_spmd as _run

    nc = _bacc.Bacc("TRN2", target_bir_lowering=False, num_devices=1)
    arrays, args = {}, {}
    for name in _INS:
        a = _np.ascontiguousarray(inputs[name])
        arrays[f"in_{name}"] = a
        args[name] = nc.dram_tensor(f"in_{name}", a.shape, _mybir.dt.from_np(a.dtype), kind="ExternalInput").ap()
    L = inputs["w_in"].shape[0]
    outs = [("y_prompt", (1, 512, 1024)), ("y_sample", (1, 32, 1024)), ("prompt_k", (L, 1, 512, 16, 64)),
            ("prompt_v", (L, 1, 512, 8, 128)), ("prompt_conv", (L, 1, 3, 1024)), ("prompt_lru", (L, 1, 1024)),
            ("sample_k", (L, 1, 32, 16, 64)), ("sample_v", (L, 1, 32, 8, 128)), ("sample_conv", (L, 1, 3, 1024)),
            ("sample_lru", (L, 1, 1024))]
    out = {name: nc.dram_tensor(f"out_{name}", shape, _mybir.dt.float32, kind="ExternalOutput").ap() for name, shape in outs}
    hybrid_encoder(nc, args, out)
    r = _run(nc, [arrays], core_ids=[0])
    return tuple(r.results[0][f"out_{name}"] for name, _ in outs)
```
